# Optimizing a Trainium2 kernel written in Bass

```python
import jax, jax.numpy as jnp
from jax import lax
import numpy as np

D_MODEL = 1024
BATCH = 1
SEQ = 256
DEPTH = 1

D_MIX = D_MODEL
D_POOL = D_MIX // 2
POOL_WINDOWS = (2, 4, 8, 16)
N_POOL_GROUPS = len(POOL_WINDOWS)
POOL_GROUP = D_POOL // N_POOL_GROUPS
D_ATTN = D_MIX - D_POOL
HEAD_DIM = 64
N_HEADS = D_ATTN // HEAD_DIM
DILATED_PATTERNS = ((128, 1), (512, 4), (2048, 16))
Q_BLOCK = 128
N_EXPERTS = 32
TOP_K = 4
D_EXPERT = D_MODEL
SWIGLU_LIMIT = 7.0
SWIGLU_ALPHA = 1.702
EPS = 1e-5
NEG_INF = -1e30

kernel_name = 'hybrid_pool_dilated_attn_moe'

def rmsnorm(x, g):
    xf = x.astype(jnp.float32)
    y = xf * lax.rsqrt(jnp.mean(xf * xf, axis=-1, keepdims=True) + EPS)
    return (y * g.astype(jnp.float32)).astype(x.dtype)

def causal_multiscale_pool(u, w_pool, pool_scale):
    B, S, _ = u.shape
    uf = u.astype(jnp.float32)
    cs = jnp.concatenate([jnp.zeros((B, 1, D_POOL), jnp.float32), jnp.cumsum(uf, axis=1)], axis=1)
    t = jnp.arange(S)
    groups = []
    for gi, w in enumerate(POOL_WINDOWS):
        lo, hi = gi * POOL_GROUP, (gi + 1) * POOL_GROUP
        start = jnp.maximum(t + 1 - w, 0)
        csg = cs[:, :, lo:hi]
        win_sum = csg[:, 1:] - csg[:, start]
        count = (t + 1 - start).astype(jnp.float32)[None, :, None]
        groups.append(win_sum / count - uf[:, :, lo:hi])
    pooled = jnp.stack(groups, axis=2)
    y = jnp.einsum('bsgc,gcd->bsgd', pooled, w_pool.astype(jnp.float32)).reshape(B, S, D_POOL)
    return (y * pool_scale.astype(jnp.float32)).astype(u.dtype)

def dilated_branch(q, k, v, window, dilation):
    B, H, S, hd = q.shape
    n_back = window // dilation
    Lc = S // dilation
    nb = -(-Lc // Q_BLOCK)
    Lp = nb * Q_BLOCK

    def compress(a):
        a = a.reshape(B, H, Lc, dilation, hd).transpose(0, 1, 3, 2, 4)
        return jnp.pad(a, ((0, 0), (0, 0), (0, 0), (0, Lp - Lc), (0, 0)))

    def slabs(a):
        a = jnp.pad(a, ((0, 0), (0, 0), (0, 0), (Q_BLOCK, 0), (0, 0)))
        a = a.reshape(B, H, dilation, nb + 1, Q_BLOCK, hd)
        return jnp.concatenate([a[:, :, :, :-1], a[:, :, :, 1:]], axis=4)

    qb = compress(q).reshape(B, H, dilation, nb, Q_BLOCK, hd)
    ks = slabs(compress(k))
    vs = slabs(compress(v))
    s = jnp.einsum('bhrnqe,bhrnke->bhrnqk', qb, ks, preferred_element_type=jnp.float32)
    qi = jnp.arange(Q_BLOCK)[:, None]
    kj = jnp.arange(2 * Q_BLOCK)[None, :]
    diff = qi + Q_BLOCK - kj
    band = (diff >= 0) & (diff <= n_back)
    key_pos = (jnp.arange(nb)[:, None, None] - 1) * Q_BLOCK + kj[None]
    mask = band[None] & (key_pos >= 0)
    s = jnp.where(mask, s, NEG_INF)
    m = jnp.max(s, axis=-1, keepdims=True)
    p = jnp.exp(s - m)
    l = jnp.sum(p, axis=-1)
    o = jnp.einsum('bhrnqk,bhrnke->bhrnqe', p, vs.astype(jnp.float32)) / l[..., None]

    def uncompress(a, tail):
        a = a.reshape((B, H, dilation, Lp) + tail)[:, :, :, :Lc]
        a = jnp.moveaxis(a, 2, 3)
        return a.reshape((B, H, S) + tail)

    return uncompress(o, (hd,)), uncompress(m[..., 0], ()), uncompress(l, ())

def dilated_attention(q, k, v):
    outs = [dilated_branch(q, k, v, w, d) for (w, d) in DILATED_PATTERNS]
    m_all = outs[0][1]
    for _, m_i, _ in outs[1:]:
        m_all = jnp.maximum(m_all, m_i)
    wts = [l_i * jnp.exp(m_i - m_all) for (_, m_i, l_i) in outs]
    total = wts[0] + wts[1] + wts[2]
    o = (wts[0][..., None] * outs[0][0] + wts[1][..., None] * outs[1][0]
         + wts[2][..., None] * outs[2][0]) / total[..., None]
    return o

def moe_ffn(h, w_router, b_router, w_gu, b_gu, w_down, b_down):
    B, S, D = h.shape
    t = h.reshape(B * S, D)
    logits = (jnp.dot(t, w_router, preferred_element_type=jnp.float32) + b_router.astype(jnp.float32))
    top_vals, top_idx = lax.top_k(logits, TOP_K)
    gates = jax.nn.softmax(top_vals, axis=-1)
    combine = jnp.sum(jax.nn.one_hot(top_idx, N_EXPERTS, dtype=jnp.float32) * gates[..., None], axis=1)
    out = jnp.zeros((B * S, D), jnp.float32)
    for e in range(N_EXPERTS):
        gu = jnp.dot(t, w_gu[e], preferred_element_type=jnp.float32) + b_gu[e].astype(jnp.float32)
        gate = jnp.minimum(gu[:, :D_EXPERT], SWIGLU_LIMIT)
        lin = jnp.clip(gu[:, D_EXPERT:], -SWIGLU_LIMIT, SWIGLU_LIMIT)
        act = gate * jax.nn.sigmoid(SWIGLU_ALPHA * gate) * (lin + 1.0)
        y = jnp.dot(act.astype(h.dtype), w_down[e], preferred_element_type=jnp.float32) + b_down[e].astype(jnp.float32)
        out = out + combine[:, e:e + 1] * y
    return out.reshape(B, S, D).astype(h.dtype)

def setup_inputs(seed: int = 0) -> dict:
    key = jax.random.key(seed)
    ks = jax.random.split(key, 14)
    f32 = jnp.float32
    d_in = D_POOL + 3 * D_ATTN
    nrm = lambda k, shape, scale: jax.random.normal(k, shape, f32) * scale
    return {
        'x': nrm(ks[0], (BATCH, SEQ, D_MODEL), 1.0),
        'g_mix': 1.0 + nrm(ks[1], (DEPTH, D_MODEL), 0.02),
        'w_in': nrm(ks[2], (DEPTH, D_MODEL, d_in), D_MODEL ** -0.5),
        'w_pool': nrm(ks[3], (DEPTH, N_POOL_GROUPS, POOL_GROUP, POOL_GROUP), POOL_GROUP ** -0.5),
        'pool_scale': 1.0 + nrm(ks[4], (DEPTH, D_POOL), 0.02),
        'w_out': nrm(ks[5], (DEPTH, D_MIX, D_MODEL), D_MIX ** -0.5),
        'g_ffn': 1.0 + nrm(ks[6], (DEPTH, D_MODEL), 0.02),
        'w_router': nrm(ks[7], (DEPTH, D_MODEL, N_EXPERTS), D_MODEL ** -0.5),
        'b_router': nrm(ks[8], (DEPTH, N_EXPERTS), 0.01),
        'w_gu': nrm(ks[9], (DEPTH, N_EXPERTS, D_MODEL, 2 * D_EXPERT), D_MODEL ** -0.5),
        'b_gu': nrm(ks[10], (DEPTH, N_EXPERTS, 2 * D_EXPERT), 0.01),
        'w_down': nrm(ks[11], (DEPTH, N_EXPERTS, D_EXPERT, D_MODEL), D_EXPERT ** -0.5),
        'b_down': nrm(ks[12], (DEPTH, N_EXPERTS, D_MODEL), 0.01),
        'g_final': 1.0 + nrm(ks[13], (D_MODEL,), 0.02),
    }

def reference(x, g_mix, w_in, w_pool, pool_scale, w_out, g_ffn, w_router, b_router,
              w_gu, b_gu, w_down, b_down, g_final):
    B, S, _ = x.shape

    def heads(a):
        return a.reshape(B, S, N_HEADS, HEAD_DIM).transpose(0, 2, 1, 3)

    for layer in range(DEPTH):
        h = rmsnorm(x, g_mix[layer])
        proj = jnp.dot(h, w_in[layer], preferred_element_type=jnp.float32).astype(x.dtype)
        u = proj[..., :D_POOL]
        q = heads(proj[..., D_POOL:D_POOL + D_ATTN]) * (HEAD_DIM ** -0.5)
        k = heads(proj[..., D_POOL + D_ATTN:D_POOL + 2 * D_ATTN])
        v = heads(proj[..., D_POOL + 2 * D_ATTN:])
        y_pool = causal_multiscale_pool(u, w_pool[layer], pool_scale[layer])
        y_attn = dilated_attention(q, k, v).transpose(0, 2, 1, 3).reshape(B, S, D_ATTN).astype(x.dtype)
        mixed = jnp.concatenate([y_pool, y_attn], axis=-1)
        x = x + jnp.dot(mixed, w_out[layer], preferred_element_type=jnp.float32).astype(x.dtype)
        h2 = rmsnorm(x, g_ffn[layer])
        x = x + moe_ffn(h2, w_router[layer], b_router[layer], w_gu[layer], b_gu[layer],
                        w_down[layer], b_down[layer])
    return rmsnorm(x, g_final)


_drawn_inputs = setup_inputs


def setup_inputs(seed=0):
    import zlib

    import numpy as np

    out = dict(_drawn_inputs(seed))
    spreads = {}
    factors = {'b_gu': 8.0, 'b_down': 8.0, 'g_final': 2.745}
    for name, (base, spread) in spreads.items():
        noise = np.random.default_rng([zlib.crc32(name.encode()), seed]).standard_normal(out[name].shape)
        drawn = base * np.exp(spread * noise) if base else spread * noise
        out[name] = __import__('jax').numpy.asarray(drawn.astype(out[name].dtype))
    for name, factor in factors.items():
        out[name] = (out[name] * factor).astype(out[name].dtype)
    return out
```

```python
from contextlib import ExitStack

import concourse.bass as bass
import numpy as np
from concourse import mybir

F32 = mybir.dt.float32
F32R = mybir.dt.float32r
I32 = mybir.dt.int32
U32 = mybir.dt.uint32
ALU = mybir.AluOpType
ACT = mybir.ActivationFunctionType
AX = mybir.AxisListType

P = 128
T, D = 256, 1024
TT = T // P
DC = D // P
DP = 512
DA = 512
H, HD = 8, 64
WINDOWS = (2, 4, 8, 16)
PATTERNS = ((128, 1), (512, 4), (2048, 16))
E, K, FE = 32, 4, 1024
LIMIT, ALPHA, EPS = 7.0, 1.702, 1e-5
NEG = -1e30
SLOTS = 64
PAD = 16
N_IN = DP + 3 * DA

UW = 2048
RAW = 8
SPL = 3
GU_U, DN_U = 8, 4
ITER_U = 2 * (GU_U + DN_U)
PRE_U = GU_U
PAIRS = E // 2

_AT, _n = {}, 0
for _name, _w in (("ident", P), ("earlier", P), ("ones", P), ("stack", SLOTS), ("slots", SLOTS), ("experts", E),
                  ("limits", 4), ("selsrc", E), ("count0", P), ("count1", 2 * P), ("invcount", 4 * PAD)):
    _AT[_name] = (_n, _n + _w)
    _n += _w
N_CONST = _n


def constants():
    c = np.zeros((P, N_CONST), np.float32)

    def put(name, a):
        lo, hi = _AT[name]
        c[:a.shape[0], lo:hi] = a

    r = np.arange(P)
    put("ident", np.eye(P))
    put("earlier", r[:, None] < r[None, :])
    put("ones", np.ones((P, P)))
    put("stack", np.concatenate([np.eye(SLOTS)] * 2))
    put("slots", np.tile(np.arange(SLOTS), (P, 1)))
    put("experts", np.tile(np.arange(E), (P, 1)))
    put("limits", np.tile([SLOTS, 2 * SLOTS, 3 * SLOTS, T], (P, 1)))
    put("selsrc", np.concatenate([np.eye(E)] * 2))
    diff = np.arange(T)[:, None] - np.arange(T)[None, :]
    seen = sum(((diff >= 0) & (diff % d == 0) & (diff // d <= w // d)).astype(np.float32) for w, d in PATTERNS)
    put("count0", seen[:P, :P])
    put("count1", seen[P:])
    put("invcount", np.tile(np.concatenate([1.0 / np.minimum(np.arange(PAD) + 1.0, w) for w in WINDOWS]), (P, 1)))
    return c


def hybrid_layer(nc, x, g_mix, w_in, w_pool, pool_scale, w_out, g_ffn, w_router, b_router,
                 w_gu, b_gu, w_down, b_down, g_final, consts, out):
    KB = 1024
    with ExitStack() as ctx:
        def sem(name):
            return ctx.enter_context(nc.semaphore(name))

        base = (nc.sbuf_base + 31) // 32 * 32
        arena_bytes = 207 * KB + 768
        ctx.enter_context(nc.sbuf_tensor("arena", [P, arena_bytes // 4], F32))

        def at(name, shape, dt, off):
            size = 4
            for s in shape[1:]:
                size *= s
            assert off + size <= arena_bytes, (name, off, size)
            return nc.alloc_sbuf_tensor_at(name, shape, dt, offset=base + off)

        raw = at("raw", [P, RAW, UW], F32, 0)
        split = at("split", [P, SPL, 2, UW], F32R, 64 * KB)
        xT = at("xT", [P, 2, DC, 2, SLOTS], F32R, 112 * KB)
        gu = at("gu", [P, 2 * FE], F32, 120 * KB)
        gate = at("gate", [P, DC * SLOTS], F32, 128 * KB)
        sig = at("sig", [P, DC * SLOTS], F32, 130 * KB)
        lin = at("lin", [P, DC * SLOTS], F32, 132 * KB)
        gsig = at("gsig", [P, DC * SLOTS], F32, 134 * KB)
        actv = at("actv", [P, DC * SLOTS], F32, 136 * KB)
        actT = at("actT", [P, DC, 2, SLOTS], F32R, 138 * KB)
        ysc = at("ysc", [P, 2, D], F32, 142 * KB)
        disp = at("disp", [P, TT, 2, 2, SLOTS], F32R, 150 * KB)
        dispT = at("dispT", [P, 2, TT, P], F32, 152 * KB)
        h2h = at("h2h", [P, TT, D], F32R, 154 * KB)
        h2l = at("h2l", [P, TT, D], F32R, 162 * KB)
        acc = at("acc", [P, TT, D], F32, 170 * KB)
        bgu = at("bgu", [2 * E, 2 * FE], F32R, 178 * KB)
        gfin = at("gfin", [P, D], F32, 186 * KB)
        outs = at("outs", [P, TT, D], F32, 0)
        junk3 = [at(f"junk3{t}", [P, D], F32, (8 + 4 * t) * KB) for t in range(TT)]
        wout = at("wout", [P, DC, D], F32, 64 * KB)
        xr = at("xr", [P, TT, D], F32, 96 * KB)
        hT = at("hT", [P, DC, T], F32, 104 * KB)
        sm1 = at("sm1", [P, H, 2 * P], F32, 96 * KB)
        pr1 = at("pr1", [P, H, 2 * P], F32, 104 * KB)
        h2 = at("h2", [P, TT, D], F32, 96 * KB)
        h2T = at("h2T", [P, DC, T], F32, 104 * KB)
        junk = [at(f"junk{t}", [P, D], F32, (112 + 4 * t) * KB) for t in range(TT)]
        qT = at("qT", [P, 4, T], F32, 112 * KB)
        kT = at("kT", [P, 4, T], F32, 116 * KB)
        braw = at("braw", [2 * E, 2 * FE], F32, 120 * KB)
        sm0 = at("sm0", [P, H, P], F32, 120 * KB)
        pr0 = at("pr0", [P, H, P], F32, 124 * KB)
        W = PAD + T
        uT = at("uT", [P, 4, W], F32, 128 * KB)
        wsA = at("wsA", [P, 4, W], F32, 128 * KB + 16 * W)
        wsB = at("wsB", [P, 4, W], F32, 128 * KB + 32 * W)
        assert 48 * W <= 13 * KB
        wrt = at("wrt", [P, DC, E], F32, 141 * KB)
        gffn = at("gffn", [P, D], F32, 146 * KB)
        neg0 = at("neg0", [P, P], F32, 150 * KB)
        neg1 = at("neg1", [P, 2 * P], F32, 150 * KB + 512)
        vecs = at("vecs", [DC + 4, P], F32, 151 * KB + 512)
        wpool = at("wpool", [P, 4, P], F32, 152 * KB)
        prT = at("prT", [P, 3 * H, P], F32, 154 * KB)
        yat = at("yat", [P, TT, DA], F32, 166 * KB)
        mixT = at("mixT", [P, DC, T], F32, 190 * KB)
        vau = at("vau", [P, TT, H, HD + 1], F32, 198 * KB)

        top = [0]

        def small(name, shape, dt=F32):
            size = 4
            for s in shape[1:]:
                size *= s
            top[0] += (size + 31) // 32 * 32
            return at(name, shape, dt, top[0] - (size + 31) // 32 * 32)

        top[0] = 198 * KB + 4 * TT * H * (HD + 1)
        cst = small("cst", [P, N_CONST])
        brt = small("brt", [P, E])
        vecT = small("vecT", [P, DC + 4])
        identr = small("identr", [P, P], F32R)
        ssq = small("ssq", [P, TT])
        inv = small("inv", [P, TT])
        rs = small("rs", [P, TT])
        mxs = small("mxs", [P, 2, H])
        nmx = small("nmx", [P, 2, H])
        rden = small("rden", [P, 2, H])
        top[0] = 190 * KB
        onehot = small("onehot", [P, TT, K, E])
        weighted = small("weighted", [P, TT, K, E])
        lg = small("lg", [P, TT, E])
        v8 = small("v8", [P, TT, 8])
        i8 = small("i8", [P, TT, 8], U32)
        i4 = small("i4", [P, TT, K])
        nv1 = small("nv1", [P, TT])
        e4 = small("e4", [P, TT, K])
        s4 = small("s4", [P, TT])
        r4 = small("r4", [P, TT])
        g4 = small("g4", [P, TT, K])
        mask = small("mask", [P, TT, E])
        comb = small("comb", [P, TT, E])
        rank1 = small("rank1", [P, TT, E])
        rank = small("rank", [P, TT, E])
        most = small("most", [P, 1])
        over = small("over", [P, 4])
        nover = small("nover", [P, 1])
        further = small("further", [P, 1], I32)
        cpair = small("cpair", [P, TT, 2])
        gslot = small("gslot", [P, 2])
        sel = small("sel", [2 * E, 2, 2, SLOTS], F32R)

        ps = ctx.enter_context(nc.psum_tensor("ps", [P, 8, 512], F32))
        GU, Y = 0, 4
        M = (6, 7)

        def c_(name, rows=P):
            lo, hi = _AT[name]
            return cst[0:rows, lo:hi]

        def bc(ap, *dims):
            return ap.broadcast_to(list(dims))

        x_loaded = [sem(f"x_loaded{t}") for t in range(TT)]
        raw_loaded = [sem(f"raw_loaded{s}") for s in range(RAW)]
        const_loaded, vec_loaded, wout_loaded = sem("const_loaded"), sem("vec_loaded"), sem("wout_loaded")
        wpool_loaded, router_loaded = sem("wpool_loaded"), sem("router_loaded")
        bgu_loaded, bdown_loaded = sem("bgu_loaded"), sem("bdown_loaded")
        gffn_loaded, gfin_loaded = sem("gffn_loaded"), sem("gfin_loaded")
        stored = sem("stored")
        squares, inv_ready, rstd_ready, scaled = sem("squares"), sem("inv_ready"), sem("rstd_ready"), sem("scaled")
        dve_step, pool_step = sem("dve_step"), sem("pool_step")
        vec_turned, vec_ready = sem("vec_turned"), sem("vec_ready")
        x_turned, hT_act, hT_dve = sem("x_turned"), sem("hT_act"), sem("hT_dve")
        win_used, q_ready, k_ready, u_ready, v_ready = (
            sem("win_used"), sem("q_ready"), sem("k_ready"), sem("u_ready"), sem("v_ready"))
        pads_ready, pooled_ready, ypool_done, ypool_ready = (
            sem("pads_ready"), sem("pooled_ready"), sem("ypool_done"), sem("ypool_ready"))
        scores, masked, max_ready, exp_done, probs = (
            sem("scores"), sem("masked"), sem("max_ready"), sem("exp_done"), sem("probs"))
        probs_turned, prT_act, prT_dve, attended, yat_ready, yat_turned, ymix_ready = (
            sem("probs_turned"), sem("prT_act"), sem("prT_dve"), sem("attended"), sem("yat_ready"),
            sem("yat_turned"), sem("ymix_ready"))
        projected, h2_turned, h2T_act, h2T_dve, logits = (
            sem("projected"), sem("h2_turned"), sem("h2T_act"), sem("h2T_dve"), sem("logits"))
        h2h_ready, h2l_ready, bgu_high, bgu_ready, identr_ready = (
            sem("h2h_ready"), sem("h2l_ready"), sem("bgu_high"), sem("bgu_ready"), sem("identr_ready"))
        top_ready, exp4_done, mask_ready, ranked, comb_ready, comb_turned = (
            sem("top_ready"), sem("exp4_done"), sem("mask_ready"), sem("ranked"), sem("comb_ready"),
            sem("comb_turned"))
        combT_ready, rounds_ready, ysc_zeroed, dispT_zeroed = (
            sem("combT_ready"), sem("rounds_ready"), sem("ysc_zeroed"), sem("dispT_zeroed"))
        high_ready, low_ready, unit_used = sem("high_ready"), sem("low_ready"), sem("unit_used")
        sel_zeroed, sel_ready, bias_added = sem("sel_zeroed"), sem("sel_ready"), sem("bias_added")
        gu_copied, outputs_ready = sem("gu_copied"), sem("outputs_ready")
        gate_turned, up_turned, gate_clipped, up_clipped = (
            sem("gate_turned"), sem("up_turned"), sem("gate_clipped"), sem("up_clipped"))
        sig_done, gsig_done, act_done, act_high, act_ready = (
            sem("sig_done"), sem("gsig_done"), sem("act_done"), sem("act_high"), sem("act_ready"))
        disp_ready, gathered, xT_ready = sem("disp_ready"), sem("gathered"), sem("xT_ready")
        disp_turned, dispT_ready, slots_gated, gslot_ready = (
            sem("disp_turned"), sem("dispT_ready"), sem("slots_gated"), sem("gslot_ready"))
        scattered, added, pair_taken = sem("scattered"), sem("added"), sem("pair_taken")

        def pair_of(i):
            return i % PAIRS

        block = ctx.enter_context(nc.Block())

        @block.sync
        def _(sp):
            for t in range(TT):
                sp.dma_start(acc[:, t, :], x[0, t * P:(t + 1) * P, :]).then_inc(x_loaded[t], 16)
            sp.dma_start(cst[:], consts).then_inc(const_loaded, 16)
            for c in range(DC):
                sp.dma_start(raw[:, c, :], w_in[0, c * P:(c + 1) * P, :]).then_inc(raw_loaded[c], 16)
            sp.dma_start(wout[:], w_out[0].rearrange("(c p) n -> p c n", p=P)).then_inc(wout_loaded, 16)

            def load(e, first, slot_unit):
                s = slot_unit % RAW
                if first < GU_U:
                    src = w_gu[0, bass.ds(e, 1), first * P:(first + 1) * P, :].rearrange("a p n -> p (a n)")
                    sp.dma_start(raw[:, s, :], src).then_inc(raw_loaded[s], 16)
                else:
                    u = first - GU_U
                    src = w_down[0, bass.ds(e, 1), 2 * u * P:2 * (u + 1) * P, :].rearrange(
                        "a (r p) n -> p (a r) n", p=P)
                    dst = raw[:, s, :].rearrange("p (r n) -> p r n", r=2)
                    sp.dma_start(dst, src).then_inc(raw_loaded[s], 16)

            for c in range(PRE_U):
                sp.wait_ge(win_used, c + 1)
                load(0, c, c)
            sp.wait_ge(rounds_ready, 1)
            last_pair = sp.snap(sp.value_load(further[0:1, 0:1], min_val=0, max_val=T // SLOTS - 1) * PAIRS + (PAIRS - 1))

            def iteration(i, last):
                a = pair_of(i) * 2
                nxt = pair_of(i + 1) * 2
                for k in range(ITER_U):
                    if last and k in range(GU_U + DN_U, 2 * GU_U + DN_U):
                        continue
                    at_ = k - (GU_U if last and k >= 2 * GU_U + DN_U else 0)
                    sp.wait_ge(low_ready, i * ITER_U + at_ + 1)
                    if k < GU_U:
                        load(a + 1, k, at_)
                    elif k < GU_U + DN_U:
                        load(a, k, at_)
                    elif k < 2 * GU_U + DN_U:
                        load(nxt, k - GU_U - DN_U, at_)
                    else:
                        load(a + 1, k - GU_U - DN_U, at_)

            with sp.Fori(0, last_pair) as i:
                iteration(i, False)
            iteration(last_pair, True)
            sp.wait_ge(scaled, 3 * TT)
            sp.dma_start(out[0].rearrange("(t p) n -> p t n", p=P), outs[:]).then_inc(stored, 16)
            sp.wait_ge(stored, 16)

        @block.gpsimd
        def _(pool):
            steps = [0]

            def link(ins):
                steps[0] += 1
                ins.then_inc(pool_step, 1)
                pool.wait_ge(pool_step, steps[0])

            pool.memset(uT[:, :, 0:PAD], 0.0).then_inc(pads_ready, 1)
            pool.memset(vau[:, :, :, HD:HD + 1], 1.0).then_inc(pads_ready, 1)
            pool.memset(ysc[:, 0, :], 0.0).then_inc(ysc_zeroed, 1)
            pool.wait_ge(const_loaded, 16)
            pool.wait_ge(u_ready, 1)
            pool.wait_ge(pads_ready, 2)
            link(pool.tensor_tensor(wsA[:, :, 1:W], uT[:, :, 1:W], uT[:, :, 0:W - 1], ALU.add))
            link(pool.tensor_tensor(wsB[:, 1:4, 3:W], wsA[:, 1:4, 3:W], wsA[:, 1:4, 1:W - 2], ALU.add))
            link(pool.tensor_tensor(wsA[:, 2:4, 7:W], wsB[:, 2:4, 7:W], wsB[:, 2:4, 3:W - 4], ALU.add))
            link(pool.tensor_tensor(wsB[:, 3:4, 15:W], wsA[:, 3:4, 15:W], wsA[:, 3:4, 7:W - 8], ALU.add))
            for g, w in enumerate(WINDOWS):
                ws = (wsA, wsB)[g % 2]
                pool.tensor_tensor(mixT[:, 4 + g, 0:PAD], ws[:, g, PAD:2 * PAD],
                                   c_("invcount")[:, g * PAD:(g + 1) * PAD], ALU.mult)
                ins = pool.tensor_scalar(mixT[:, 4 + g, PAD:T], ws[:, g, 2 * PAD:W], 1.0 / w, None, ALU.mult)
            link(ins)
            pool.tensor_tensor(mixT[:, 4:8, :], mixT[:, 4:8, :], uT[:, :, PAD:W], ALU.subtract).then_inc(pooled_ready, 1)
            pool.wait_ge(projected, 2)
            pool.memset(sel[:].bitcast(F32), 0.0).then_inc(sel_zeroed, 1)
            pool.wait_ge(ypool_done, 1)
            pool.memset(dispT[:], 0.0).then_inc(dispT_zeroed, 1)
            pool.wait_ge(scaled, 2 * TT)
            pool.memset(ysc[:, 1, :], 0.0).then_inc(ysc_zeroed, 1)
            pool.wait_ge(rounds_ready, 1)
            last_pair = pool.snap(pool.value_load(further[0:1, 0:1], min_val=0, max_val=T // SLOTS - 1) * PAIRS + (PAIRS - 1))

            def select(e, half):
                src = c_("selsrc", 2 * E)[:, bass.ds(e, 1)]
                pool.wait_ge(sel_zeroed, 1)
                pool.tensor_tensor(sel[:, half, 0, :], bc(src, 2 * E, SLOTS), c_("ones", 2 * E)[:, 0:SLOTS],
                                   ALU.mult).then_inc(sel_ready, 1)

            select(0, 0)
            with pool.Fori(0, last_pair) as i:
                pool.wait_ge(bias_added, i * 2 + 1)
                select(pair_of(i) * 2 + 1, 1)
                pool.wait_ge(bias_added, i * 2 + 1)
                select(pair_of(i + 1) * 2, 0)
            i = last_pair
            pool.wait_ge(bias_added, i * 2 + 1)
            select(pair_of(i) * 2 + 1, 1)

        @block.scalar
        def _(act):
            act.dma_start(vecs[0:DC, :], g_mix.rearrange("a (c p) -> (a c) p", p=P)).then_inc(vec_loaded, 16)
            act.dma_start(vecs[DC:DC + 4, :], pool_scale.rearrange("a (c p) -> (a c) p", p=P)).then_inc(vec_loaded, 16)
            act.dma_start(wpool[:], w_pool[0].rearrange("g c d -> c g d")).then_inc(wpool_loaded, 16)
            for part in range(2):
                act.dma_start(braw[part * E:(part + 1) * E, :], b_gu[0]).then_inc(bgu_loaded, 16)
            act.dma_start(wrt[:], w_router[0].rearrange("(c p) e -> p c e", p=P)).then_inc(router_loaded, 16)
            act.dma_start(brt[:], b_router.broadcast_to([P, E])).then_inc(router_loaded, 16)
            act.dma_start(gffn[:], g_ffn.broadcast_to([P, D])).then_inc(gffn_loaded, 16)
            act.dma_start(gfin[:], g_final.rearrange("(a n) -> a n", a=1).broadcast_to([P, D])).then_inc(gfin_loaded, 16)
            act.wait_ge(ysc_zeroed, 1)
            act.dma_start(ysc[0:E, 0, :], b_down[0]).then_inc(bdown_loaded, 16)

            def norm(n, squares_of):
                for t in range(TT):
                    act.activation(squares_of[t][:], acc[:, t, :], ACT.Square, accum_out=ssq[:, t:t + 1]).then_inc(squares, 1)
                act.wait_ge(inv_ready, n + 1)
                act.activation(rs[:], inv[:], ACT.Sqrt).then_inc(rstd_ready, 1)

            for t in range(TT):
                act.wait_ge(x_loaded[t], 16)
            norm(0, junk)
            act.wait_ge(vec_ready, 1)
            for b in range(2):
                act.wait_ge(x_turned, b + 1)
                for c in (2 * b, 2 * b + 1):
                    ins = act.activation(hT[:, c, :], ps[:, b, (c % 2) * T:(c % 2 + 1) * T], ACT.Copy,
                                         scale=vecT[:, c:c + 1])
                ins.then_inc(hT_act, 1)
            act.wait_ge(bgu_loaded, 32)
            act.activation(bgu[:], braw[:], ACT.Copy).then_inc(bgu_high, 1)
            act.wait_ge(const_loaded, 16)
            act.activation(identr[:], c_("ident"), ACT.Copy).then_inc(identr_ready, 1)
            act.wait_ge(win_used, DC)
            act.activation(qT[:].rearrange("p c t -> p (c t)"), ps[:, 0:2, :].rearrange("p a b -> p (a b)"),
                           ACT.Copy).then_inc(q_ready, 1)
            act.activation(uT[:, :, PAD:W], ps[:, 4:6, :].rearrange("p a (b t) -> p (a b) t", b=2),
                           ACT.Copy).then_inc(u_ready, 1)

            def exps(tile, pr, sm):
                act.wait_ge(max_ready, tile + 1)
                for s in range(H):
                    ins = act.activation(pr[:, s, :], sm[:, s, :], ACT.Exp, bias=nmx[:, tile, s:s + 1])
                ins.then_inc(exp_done, 1)

            exps(0, pr1, sm1)
            act.wait_ge(ypool_done, 1)
            for g in range(4):
                ins = act.activation(mixT[:, g, :], ps[:, 6 + g // 2, (g % 2) * T:(g % 2 + 1) * T], ACT.Copy,
                                     scale=vecT[:, DC + g:DC + g + 1])
            ins.then_inc(ypool_ready, 1)
            exps(1, pr0, sm0)
            act.wait_ge(probs_turned, 1)
            act.activation(prT[:, 0:8, :].rearrange("p a b -> p (a b)"), ps[:, 0:2, :].rearrange("p a b -> p (a b)"),
                           ACT.Copy).then_inc(prT_act, 1)
            act.wait_ge(probs_turned, 2)
            act.activation(prT[:, 16:24, :].rearrange("p a b -> p (a b)"), ps[:, 4:6, :].rearrange("p a b -> p (a b)"),
                           ACT.Copy).then_inc(prT_act, 1)
            act.wait_ge(yat_turned, 1)
            act.activation(mixT[:, 4:8, :].rearrange("p a b -> p (a b)"), ps[:, 2:4, :].rearrange("p a b -> p (a b)"),
                           ACT.Copy).then_inc(ymix_ready, 1)
            for t in range(TT):
                act.wait_ge(added, 1 + t)
            norm(1, junk)
            for b in range(2):
                act.wait_ge(h2_turned, b + 1)
                act.activation(h2T[:, 2 * b:2 * b + 2, :].rearrange("p a b -> p (a b)"), ps[:, b, :],
                               ACT.Copy).then_inc(h2T_act, 1)
            act.activation(h2h[:], h2[:], ACT.Copy).then_inc(h2h_ready, 1)
            act.wait_ge(top_ready, 1)
            for t in range(TT):
                act.activation(e4[:, t, :], v8[:, t, 0:K], ACT.Exp, bias=nv1[:, t:t + 1],
                               accum_out=s4[:, t:t + 1]).then_inc(exp4_done, 1)
            def high(n, k, first_use):
                act.wait_ge(raw_loaded[k % RAW], (first_use + 1) * 16)
                if not isinstance(n, int) or n >= SPL:
                    act.wait_ge(unit_used, n - SPL + 1)
                act.activation(split[:, k % SPL, 0, :], raw[:, k % RAW, :], ACT.Copy).then_inc(high_ready, 1)

            def gather_copy(job, count):
                act.wait_ge(gathered, count)
                act.activation(xT[:, :, 2 * job:2 * job + 2].rearrange("p e c a s -> p e (c a s)"),
                               ps[:, M[job % 2], :].rearrange("p (e n) -> p e n", e=2), ACT.Copy).then_inc(xT_ready, 1)

            def gu_copy(e, used):
                act.wait_ge(unit_used, used)
                if not isinstance(e, int):
                    act.wait_ge(up_turned, e)
                act.activation(gu[:], ps[:, 0:4, :].rearrange("p a b -> p (a b)"), ACT.Copy).then_inc(gu_copied, 1)

            def sigmoid(e):
                act.wait_ge(gate_clipped, e + 1)
                act.activation(sig[:], gate[:], ACT.Sigmoid, scale=ALPHA).then_inc(sig_done, 1)

            def act_split(e, used=None):
                act.wait_ge(act_done, e + 1)
                if used is not None:
                    act.wait_ge(unit_used, used)
                act.activation(actT[:, :, 0, :], actv[:].rearrange("p (c s) -> p c s", s=SLOTS),
                               ACT.Copy).then_inc(act_high, 1)

            def y_copy(i, half, used):
                act.wait_ge(unit_used, used)
                act.wait_ge(gslot_ready, i + 1)
                act.wait_ge(scattered, i * 4 + 4)
                act.activation(ysc[:, half, :], ps[:, Y:Y + 2, :].rearrange("p a b -> p (a b)"), ACT.Copy,
                               scale=gslot[:, half:half + 1]).then_inc(outputs_ready, 1)

            for k in range(2):
                high(k, k, 1)
            act.wait_ge(rounds_ready, 1)
            last_pair = act.snap(act.value_load(further[0:1, 0:1], min_val=0, max_val=T // SLOTS - 1) * PAIRS + (PAIRS - 1))
            high(2, 2, 1)
            for job in range(4):
                gather_copy(job, job + 1)
            for k in range(SPL, PRE_U):
                high(k, k, 1)
            gu_copy(0, PRE_U)

            def unit(i, k, skipped=0):
                k -= skipped
                high(i * ITER_U + PRE_U + k, PRE_U + k, i * (ITER_U // RAW) + 2 + k // RAW)

            unit(0, 0)
            sigmoid(0)
            unit(0, 1)

            def used(i, k):
                return i * ITER_U + (PRE_U + k)

            def iteration(i, last):
                unit(i, 2)
                act_split(i * 2)
                for k in range(3, 10):
                    unit(i, k)
                gu_copy(i * 2 + 1, used(i, GU_U))
                unit(i, 10)
                if not last:
                    gather_copy(0, i * 4 + 5)
                    gather_copy(1, i * 4 + 6)
                unit(i, 11)
                if not last:
                    unit(i, 12)
                    gather_copy(2, i * 4 + 7)
                    gather_copy(3, i * 4 + 8)
                    sigmoid(i * 2 + 1)
                    unit(i, 13)
                    y_copy(i, 0, used(i, 12))
                    unit(i, 14)
                    act_split(i * 2 + 1, used(i, 12))
                    for k in range(15, 22):
                        unit(i, k)
                    gu_copy(i * 2 + 2, used(i, 20))
                    unit(i, 22)
                    unit(i, 23)
                    unit(i, 24)
                    sigmoid(i * 2 + 2)
                    unit(i, 25)
                else:
                    sigmoid(i * 2 + 1)
                    unit(i, 20, GU_U)
                    y_copy(i, 0, used(i, 12))
                    act_split(i * 2 + 1, used(i, 12))
                    for k in range(21, 24):
                        unit(i, k, GU_U)
                y_copy(i, 1, used(i, 24 - (GU_U if last else 0)))

            with act.Fori(0, last_pair) as i:
                iteration(i, False)
            iteration(last_pair, True)
            act.wait_ge(added, last_pair * 4 + 8 + TT)
            norm(2, junk3)

        @block.vector
        def _(dve):
            steps = [0]

            def link(ins):
                steps[0] += 1
                ins.then_inc(dve_step, 1)
                dve.wait_ge(dve_step, steps[0])

            def inverse(n):
                dve.wait_ge(squares, 2 * n + 2)
                link(dve.tensor_scalar(inv[:], ssq[:], 1.0 / D, EPS, ALU.mult, ALU.add))
                dve.reciprocal(inv[:], inv[:]).then_inc(inv_ready, 1)
                dve.wait_ge(rstd_ready, n + 1)

            dve.wait_ge(const_loaded, 16)
            dve.tensor_scalar(neg0[:], c_("count0"), 0.0, NEG, ALU.is_equal, ALU.mult)
            link(dve.tensor_scalar(neg1[:], c_("count1"), 0.0, NEG, ALU.is_equal, ALU.mult))
            inverse(0)
            for t in range(TT):
                dve.tensor_scalar(xr[:, t, :], acc[:, t, :], rs[:, t:t + 1], None, ALU.mult).then_inc(scaled, 1)
            dve.wait_ge(vec_turned, 1)
            dve.tensor_copy(vecT[:], ps[:, 7, 0:DC + 4]).then_inc(vec_ready, 1)
            dve.wait_ge(vec_ready, 1)
            for b in range(2, 4):
                dve.wait_ge(x_turned, b + 1)
                for c in (2 * b, 2 * b + 1):
                    ins = dve.tensor_scalar(hT[:, c, :], ps[:, b, (c % 2) * T:(c % 2 + 1) * T], vecT[:, c:c + 1],
                                            None, ALU.mult)
                ins.then_inc(hT_dve, 1)
            dve.wait_ge(bgu_high, 1)
            dve.tensor_tensor(bgu[E:2 * E, :], braw[E:2 * E, :], bgu[E:2 * E, :].bitcast(F32),
                              ALU.subtract).then_inc(bgu_ready, 1)
            dve.wait_ge(win_used, DC)
            dve.tensor_copy(kT[:].rearrange("p c t -> p (c t)"),
                            ps[:, 2:4, :].rearrange("p a b -> p (a b)")).then_inc(k_ready, 1)
            for t in range(TT):
                ins = dve.tensor_copy(vau[:, t, :, 0:HD], ps[:, 6 + t, :].rearrange("p (h d) -> p h d", h=H))
            ins.then_inc(v_ready, 1)

            def mask_and_max(n, sm, bank, neg, keys):
                dve.wait_ge(scores, n + 1)
                dve.scalar_tensor_tensor(
                    out=sm[:], in0=ps[:, bank:bank + H * keys // 512, :].rearrange("p a (b k) -> p (a b) k", k=keys),
                    scalar=HD ** -0.5, in1=bc(neg[:].rearrange("p (a k) -> p a k", a=1), P, H, keys),
                    op0=ALU.mult, op1=ALU.add).then_inc(masked, 1)
                dve.wait_ge(masked, n + 1)
                link(dve.tensor_reduce(mxs[:, n, :], sm[:], AX.X, ALU.max))
                dve.tensor_scalar(nmx[:, n, :], mxs[:, n, :], -1.0, None, ALU.mult).then_inc(max_ready, 1)

            def times_count(n, pr, count, keys):
                dve.wait_ge(exp_done, n + 1)
                dve.tensor_tensor(pr[:], pr[:], bc(c_(count).rearrange("p (a k) -> p a k", a=1), P, H, keys),
                                  ALU.mult).then_inc(probs, 1)

            mask_and_max(0, sm1, 0, neg1, 2 * P)
            mask_and_max(1, sm0, 4, neg0, P)
            times_count(0, pr1, "count1", 2 * P)
            times_count(1, pr0, "count0", P)
            dve.wait_ge(probs_turned, 1)
            dve.tensor_copy(prT[:, 8:16, :].rearrange("p a b -> p (a b)"),
                            ps[:, 2:4, :].rearrange("p a b -> p (a b)")).then_inc(prT_dve, 1)
            for n in range(2):
                dve.wait_ge(attended, n + 1)
                o = ps[:, 6 - 6 * n:8 - 6 * n, 0:4 * (HD + 1)].rearrange("p a (h d) -> p a h d", d=HD + 1)
                link(dve.reciprocal(rden[:, n, :].rearrange("p (a h) -> p a h", a=2), o[:, :, :, HD]))
                for half in range(2):
                    r = rden[:, n, 4 * half:4 * half + 4].rearrange("p (h a) -> p h a", a=1)
                    ins = dve.tensor_tensor(
                        yat[:, 1 - n, half * 256:half * 256 + 256].rearrange("p (h d) -> p h d", d=HD),
                        o[:, half, :, 0:HD], bc(r, P, 4, HD), ALU.mult)
                ins.then_inc(yat_ready, 1)
            for t in range(TT):
                dve.wait_ge(projected, t + 1)
                dve.tensor_tensor(acc[:, t, :], ps[:, 4 + 2 * t:6 + 2 * t, :].rearrange("p a b -> p (a b)"),
                                  acc[:, t, :], ALU.add).then_inc(added, 1)
            inverse(1)
            dve.wait_ge(gffn_loaded, 16)
            for t in range(TT):
                dve.scalar_tensor_tensor(out=h2[:, t, :], in0=acc[:, t, :], scalar=rs[:, t:t + 1], in1=gffn[:],
                                         op0=ALU.mult, op1=ALU.mult).then_inc(scaled, 1)
            for b in range(2, 4):
                dve.wait_ge(h2_turned, b + 1)
                dve.tensor_copy(h2T[:, 2 * b:2 * b + 2, :].rearrange("p a b -> p (a b)"),
                                ps[:, b, :]).then_inc(h2T_dve, 1)
            dve.wait_ge(logits, 1)
            dve.wait_ge(router_loaded, 32)
            link(dve.tensor_tensor(lg[:], ps[:, 4, 0:TT * E].rearrange("p (t e) -> p t e", t=TT),
                                   bc(brt[:].rearrange("p (a e) -> p a e", a=1), P, TT, E), ALU.add))
            for t in range(TT):
                link(dve.max(v8[:, t, :], lg[:, t, :]))
                link(dve.max_index(i8[:, t, :], v8[:, t, :], lg[:, t, :]))
            dve.tensor_scalar(nv1[:], v8[:, :, 0], -1.0, None, ALU.mult).then_inc(top_ready, 1)
            link(dve.tensor_copy(i4[:], i8[:, :, 0:K]))
            link(dve.tensor_tensor(onehot[:].rearrange("p t k e -> p (t k) e"),
                                   bc(c_("experts").rearrange("p (a e) -> p a e", a=1), P, TT * K, E),
                                   bc(i4[:].rearrange("p t (k a) -> p (t k) a", a=1), P, TT * K, E), ALU.is_equal))
            dve.tensor_reduce(mask[:], onehot[:].rearrange("p t k e -> p t e k"), AX.X, ALU.add).then_inc(mask_ready, 1)
            dve.wait_ge(h2h_ready, 1)
            dve.tensor_tensor(h2l[:], h2[:], h2h[:].bitcast(F32), ALU.subtract).then_inc(h2l_ready, 1)
            dve.wait_ge(exp4_done, 2)
            link(dve.reciprocal(r4[:], s4[:]))
            link(dve.tensor_tensor(g4[:], e4[:], bc(r4[:].rearrange("p (t a) -> p t a", a=1), P, TT, K), ALU.mult))
            link(dve.tensor_tensor(weighted[:].rearrange("p t k e -> p (t k) e"),
                                   onehot[:].rearrange("p t k e -> p (t k) e"),
                                   bc(g4[:].rearrange("p t (k a) -> p (t k) a", a=1), P, TT * K, E), ALU.mult))
            dve.tensor_reduce(comb[:], weighted[:].rearrange("p t k e -> p t e k"), AX.X, ALU.add).then_inc(comb_ready, 1)
            dve.wait_ge(ranked, 1)
            dve.wait_ge(mask_ready, 1)
            link(dve.scalar_tensor_tensor(out=rank1[:], in0=ps[:, 5, 0:TT * E].rearrange("p (t e) -> p t e", t=TT),
                                          scalar=1.0, in1=mask[:], op0=ALU.add, op1=ALU.mult))
            link(dve.tensor_scalar(rank[:], rank1[:], -1.0, None, ALU.add))
            link(dve.tensor_reduce(most[:], ps[:, 5, TT * E:TT * E + E], AX.X, ALU.max))
            link(dve.tensor_scalar(over[:], c_("limits"), most[:, 0:1], None, ALU.is_lt))
            link(dve.tensor_reduce(nover[:], over[:], AX.X, ALU.add))
            dve.tensor_copy(further[:], nover[:]).then_inc(rounds_ready, 1)

            def build_disp(e):
                for t in range(TT):
                    mine = rank[:, t, bass.ds(e, 2)].rearrange("p (a b) -> p a b", b=1)
                    for copy in range(2):
                        ins = dve.tensor_tensor(disp[:, t, :, copy, :],
                                                bc(c_("slots").rearrange("p (a s) -> p a s", a=1), P, 2, SLOTS),
                                                bc(mine, P, 2, SLOTS), ALU.is_equal)
                ins.then_inc(disp_ready, 1)

            def next_round(e, count):
                dve.tensor_copy(cpair[:], comb[:, :, bass.ds(e, 2)])
                dve.wait_ge(disp_ready, count)
                dve.tensor_scalar(rank[:, :, bass.ds(e, 2)], rank[:, :, bass.ds(e, 2)], -float(SLOTS), None,
                                  ALU.add).then_inc(pair_taken, 1)

            dve.wait_ge(comb_ready, 1)
            build_disp(0)
            next_round(0, 1)
            dve.wait_ge(rounds_ready, 1)
            last_pair = dve.snap(dve.value_load(further[0:1, 0:1], min_val=0, max_val=T // SLOTS - 1) * PAIRS + (PAIRS - 1))
            dve.wait_ge(comb_turned, 1)
            dve.wait_ge(dispT_zeroed, 1)
            dve.tensor_copy(dispT[0:E, 0, :, :], ps[0:E, 4, 0:T].rearrange("p (t q) -> p t q", t=TT)).then_inc(outputs_ready, 1)

            def low(n, k):
                dve.wait_ge(high_ready, n + 1)
                dve.tensor_tensor(split[:, k % SPL, 1, :], raw[:, k % RAW, :], split[:, k % SPL, 0, :].bitcast(F32),
                                  ALU.subtract).then_inc(low_ready, 1)

            def clip(e):
                dve.wait_ge(gate_turned, e + 1)
                dve.tensor_scalar(gate[:], ps[:, M[0], :], LIMIT, None, ALU.min).then_inc(gate_clipped, 1)
                dve.wait_ge(up_turned, e + 1)
                dve.tensor_scalar(lin[:], ps[:, M[1], :], -LIMIT, LIMIT, ALU.max, ALU.min).then_inc(up_clipped, 1)

            def swiglu(e):
                dve.wait_ge(sig_done, e + 1)
                dve.tensor_tensor(gsig[:], gate[:], sig[:], ALU.mult).then_inc(gsig_done, 1)
                dve.wait_ge(gsig_done, e + 1)
                dve.scalar_tensor_tensor(out=actv[:], in0=lin[:], scalar=1.0, in1=gsig[:], op0=ALU.add,
                                         op1=ALU.mult).then_inc(act_done, 1)

            def act_low(e):
                dve.wait_ge(act_high, e + 1)
                dve.tensor_tensor(actT[:, :, 1, :], actv[:].rearrange("p (c s) -> p c s", s=SLOTS),
                                  actT[:, :, 0, :].bitcast(F32), ALU.subtract).then_inc(act_ready, 1)

            def add_scattered(i, job):
                dve.wait_ge(scattered, i * 4 + job + 1)
                part = acc[:, job // 2, (job % 2) * 512:(job % 2 + 1) * 512]
                dve.tensor_tensor(part, ps[:, M[job % 2], :], part, ALU.add).then_inc(added, 1)

            for k in range(PRE_U):
                low(k, k)
            clip(0)

            def iteration(i, last):
                def unit(k, skipped=0):
                    low(i * ITER_U + (PRE_U + k - skipped), PRE_U + k - skipped)

                unit(0)
                swiglu(i * 2)
                unit(1)
                unit(2)
                act_low(i * 2)
                unit(3)
                add_scattered(i, 0)
                add_scattered(i, 1)
                unit(4)
                add_scattered(i, 2)
                add_scattered(i, 3)
                unit(5)
                unit(6)
                dve.wait_ge(disp_turned, i + 1)
                dve.tensor_copy(dispT[:].rearrange("p a t q -> p (a t q)"), ps[:, M[0], :]).then_inc(dispT_ready, 1)
                unit(7)
                dve.wait_ge(slots_gated, i + 1)
                dve.tensor_copy(gslot[:], ps[:, M[1], 0:2]).then_inc(gslot_ready, 1)
                if not last:
                    dve.wait_ge(pair_taken, i + 1)
                    e = dve.snap(pair_of(i + 1) * 2)
                    build_disp(e)
                    next_round(e, i + 2)
                unit(8)
                unit(9)
                unit(10)
                clip(i * 2 + 1)
                unit(11)
                if not last:
                    unit(12)
                    unit(13)
                    swiglu(i * 2 + 1)
                    unit(14)
                    unit(15)
                    act_low(i * 2 + 1)
                    for k in range(16, 23):
                        unit(k)
                    clip(i * 2 + 2)
                    unit(23)
                else:
                    swiglu(i * 2 + 1)
                    unit(20, GU_U)
                    act_low(i * 2 + 1)
                    for k in range(21, 24):
                        unit(k, GU_U)

            with dve.Fori(0, last_pair) as i:
                iteration(i, False)
            iteration(last_pair, True)
            for job in range(4):
                add_scattered(last_pair + 1, job)
            inverse(2)
            dve.wait_ge(gfin_loaded, 16)
            for t in range(TT):
                dve.scalar_tensor_tensor(out=outs[:, t, :], in0=acc[:, t, :], scalar=rs[:, t:t + 1], in1=gfin[:],
                                         op0=ALU.mult, op1=ALU.mult).then_inc(scaled, 1)

        @block.tensor
        def _(pe):
            def mm(out_, lhsT, rhs, start=True, stop=True, shared=False):
                return pe.matmul(out_, lhsT, rhs, start=start, stop=stop, skip_group_check=shared)

            pe.wait_ge(const_loaded, 16)
            pe.wait_ge(vec_loaded, 32)
            pe.transpose(ps[:, 7, 0:DC + 4], vecs[:], c_("ident", DC + 4)[:, 0:DC + 4]).then_inc(vec_turned, 1)

            def turn(src, done):
                for c in range(DC):
                    for t in range(TT):
                        ins = pe.transpose(ps[:, c // 2, (c % 2) * T + t * P:(c % 2) * T + (t + 1) * P],
                                           src[:, t, c * P:(c + 1) * P], c_("ident"))
                    if c % 2:
                        ins.then_inc(done, 1)

            pe.wait_ge(scaled, 2)
            turn(xr, x_turned)
            pe.wait_ge(hT_act, 2)
            pe.wait_ge(hT_dve, 2)
            for c in range(DC):
                pe.wait_ge(raw_loaded[c], 16)
                first, last = c == 0, c == DC - 1
                for bank, column in ((0, DP), (2, DP + DA), (4, 0)):
                    for j in range(4):
                        mm(ps[:, bank + j // 2, (j % 2) * T:(j % 2 + 1) * T],
                           raw[:, c, column + j * P:column + (j + 1) * P], hT[:, c, :],
                           start=first and j % 2 == 0, stop=last, shared=True)
                for t in range(TT):
                    ins = mm(ps[:, 6 + t, :], hT[:, c, t * P:(t + 1) * P], raw[:, c, DP + 2 * DA:N_IN],
                             start=first, stop=last)
                ins.then_inc(win_used, 1)
            pe.wait_ge(q_ready, 1)
            pe.wait_ge(k_ready, 1)
            for n, (bank, keys) in enumerate(((0, 2 * P), (4, P))):
                if n == 1:
                    pe.wait_ge(u_ready, 1)
                tile = 1 - n
                for h in range(H):
                    s = (h % 2) * 4 + h // 2
                    rows = slice((h % 2) * HD, (h % 2 + 1) * HD)
                    per = 512 // keys
                    ins = mm(ps[:, bank + s // per, (s % per) * keys:(s % per + 1) * keys],
                             qT[rows, h // 2, tile * P:(tile + 1) * P], kT[rows, h // 2, 0:keys])
                ins.then_inc(scores, 1)
            pe.wait_ge(pooled_ready, 1)
            pe.wait_ge(wpool_loaded, 16)
            pe.wait_ge(v_ready, 1)
            for g in range(4):
                ins = mm(ps[:, 6 + g // 2, (g % 2) * T:(g % 2 + 1) * T], wpool[:, g, :], mixT[:, 4 + g, :])
            ins.then_inc(ypool_done, 1)
            pe.wait_ge(probs, 1)
            for s in range(H):
                for kb in range(2):
                    j = 2 * s + kb
                    ins = pe.transpose(ps[:, j // 4, (j % 4) * P:(j % 4 + 1) * P], pr1[:, s, kb * P:(kb + 1) * P], c_("ident"))
            ins.then_inc(probs_turned, 1)
            pe.wait_ge(probs, 2)
            for s in range(H):
                ins = pe.transpose(ps[:, 4 + s // 4, (s % 4) * P:(s % 4 + 1) * P], pr0[:, s, :], c_("ident"))
            ins.then_inc(probs_turned, 1)

            def attend(tile, bank):
                for h in range(H):
                    s = (h % 2) * 4 + h // 2
                    out_ = ps[:, bank + h // 4, (h % 4) * (HD + 1):(h % 4 + 1) * (HD + 1)]
                    for kb in range(tile + 1):
                        src = 2 * s + kb if tile else 2 * H + s
                        ins = mm(out_, prT[:, src, :], vau[:, kb, h, :], start=kb == 0, stop=kb == tile)
                ins.then_inc(attended, 1)

            pe.wait_ge(prT_act, 1)
            pe.wait_ge(prT_dve, 1)
            pe.wait_ge(ypool_ready, 1)
            pe.wait_ge(pads_ready, 2)
            attend(1, 6)
            pe.wait_ge(prT_act, 2)
            attend(0, 0)
            pe.wait_ge(yat_ready, 2)
            for j in range(4):
                for t in range(TT):
                    ins = pe.transpose(ps[:, 2 + j // 2, (j % 2) * T + t * P:(j % 2) * T + (t + 1) * P],
                                       yat[:, t, j * P:(j + 1) * P], c_("ident"))
            ins.then_inc(yat_turned, 1)
            pe.wait_ge(wout_loaded, 16)
            for half in range(2):
                if half == 1:
                    pe.wait_ge(ymix_ready, 1)
                for t in range(TT):
                    for n in range(2):
                        for c in range(4 * half, 4 * half + 4):
                            ins = mm(ps[:, 4 + 2 * t + n, :], mixT[:, c, t * P:(t + 1) * P],
                                     wout[:, c, n * 512:(n + 1) * 512], start=c == 0, stop=c == DC - 1)
                    if half == 1:
                        ins.then_inc(projected, 1)
            pe.wait_ge(scaled, 4)
            turn(h2, h2_turned)
            pe.wait_ge(h2T_act, 2)
            pe.wait_ge(h2T_dve, 2)
            pe.wait_ge(router_loaded, 32)
            for t in range(TT):
                for c in range(DC):
                    ins = mm(ps[:, 4, t * E:(t + 1) * E], h2T[:, c, t * P:(t + 1) * P], wrt[:, c, :],
                             start=c == 0, stop=c == DC - 1)
            ins.then_inc(logits, 1)
            pe.wait_ge(mask_ready, 1)
            mm(ps[:, 5, 0:E], c_("earlier"), mask[:, 0, :])
            mm(ps[:, 5, E:2 * E], c_("ones"), mask[:, 0, :], stop=False)
            mm(ps[:, 5, E:2 * E], c_("earlier"), mask[:, 1, :], start=False)
            mm(ps[:, 5, 2 * E:3 * E], c_("ones"), mask[:, 0, :], stop=False)
            mm(ps[:, 5, 2 * E:3 * E], c_("ones"), mask[:, 1, :], start=False).then_inc(ranked, 1)
            pe.wait_ge(comb_ready, 1)
            for t in range(TT):
                ins = pe.transpose(ps[0:E, 4, t * P:(t + 1) * P], comb[:, t, :], c_("ident"))
            ins.then_inc(comb_turned, 1)

            def gather(job):
                bank = ps[:, M[job % 2], :].rearrange("p (e c a s) -> p c a e s", e=2, c=2, a=2)
                for c in (2 * job, 2 * job + 1):
                    for part, src in enumerate((h2h, h2l)):
                        for t in range(TT):
                            ins = mm(bank[:, c % 2, part], src[:, t, c * P:(c + 1) * P],
                                     disp[:, t, :, 0, :], start=t == 0, stop=t == TT - 1)
                ins.then_inc(gathered, 1)

            def bias(half):
                for n in range(4):
                    ins = mm(ps[:, GU + n, :], sel[:, half, :, :].rearrange("p a s -> p (a s)"),
                             bgu[:, n * 512:(n + 1) * 512], stop=False)
                ins.then_inc(bias_added, 1)

            def gu_unit(half, c, n, k):
                pe.wait_ge(low_ready, n + 1)
                for b in range(4):
                    for part in range(2):
                        ins = mm(ps[:, GU + b, :], xT[:, half, c].rearrange("p a s -> p (a s)"), split[:, k % SPL, part, b * 512:(b + 1) * 512],
                                 start=False, stop=c == GU_U - 1 and part == 1)
                ins.then_inc(unit_used, 1)

            def down_unit(u, n, k):
                pe.wait_ge(low_ready, n + 1)
                for r in range(2):
                    m = 2 * u + r
                    for b in range(2):
                        for part in range(2):
                            col = r * D + b * 512
                            ins = mm(ps[:, Y + b, :], actT[:, m, :, :].rearrange("p a s -> p (a s)"),
                                     split[:, k % SPL, part, col:col + 512],
                                     start=m == 0 and part == 0, stop=m == DC - 1 and part == 1)
                ins.then_inc(unit_used, 1)

            def turn_gu(e):
                pe.wait_ge(gu_copied, e + 1)
                for b, done in enumerate((gate_turned, up_turned)):
                    for m in range(DC):
                        ins = mm(ps[:, M[b], m * SLOTS:(m + 1) * SLOTS],
                                 gu[:, b * FE + m * P:b * FE + (m + 1) * P], c_("stack"))
                    ins.then_inc(done, 1)

            def scatter(job):
                t, n = job // 2, job % 2
                for a in range(2):
                    ins = mm(ps[:, M[job % 2], :], dispT[:, a, t, :], ysc[:, a, n * 512:(n + 1) * 512],
                             start=a == 0, stop=a == 1)
                ins.then_inc(scattered, 1)

            pe.wait_ge(rounds_ready, 1)
            last_pair = pe.snap(pe.value_load(further[0:1, 0:1], min_val=0, max_val=T // SLOTS - 1) * PAIRS + (PAIRS - 1))
            pe.wait_ge(disp_ready, 1)
            pe.wait_ge(h2h_ready, 1)
            pe.wait_ge(h2l_ready, 1)
            for job in range(4):
                if job >= 2:
                    pe.wait_ge(xT_ready, job - 1)
                gather(job)
            pe.wait_ge(xT_ready, 4)
            pe.wait_ge(sel_ready, 1)
            pe.wait_ge(bgu_ready, 1)
            bias(0)
            for c in range(GU_U):
                gu_unit(0, c, c, c)
            pe.wait_ge(bdown_loaded, 16)
            pe.wait_ge(ysc_zeroed, 2)
            pe.wait_ge(identr_ready, 1)
            turn_gu(0)

            def iteration(i, last):
                def n_(k):
                    return i * ITER_U + PRE_U + k

                pe.wait_ge(gu_copied, i * 2 + 1)
                pe.wait_ge(sel_ready, i * 2 + 2)
                bias(1)
                for k in range(GU_U):
                    gu_unit(1, k, n_(k), PRE_U + k)
                    if k == 1:
                        pe.wait_ge(outputs_ready, i * 2 + 1)
                        pe.wait_ge(gate_clipped, i * 2 + 1)
                        scatter(0)
                        pe.wait_ge(up_clipped, i * 2 + 1)
                        scatter(1)
                    if k == 2:
                        pe.wait_ge(added, i * 4 + TT + 1)
                        scatter(2)
                        pe.wait_ge(added, i * 4 + TT + 2)
                        scatter(3)
                    if k == 3:
                        pe.wait_ge(added, i * 4 + TT + 3)
                        for a in range(2):
                            for t in range(TT):
                                ins = mm(ps[:, M[0], (2 * a + t) * P:(2 * a + t + 1) * P],
                                         disp[:, t, a, :, :].rearrange("p c s -> p (c s)"), identr[:])
                        ins.then_inc(disp_turned, 1)
                    if k == 4:
                        pe.wait_ge(added, i * 4 + TT + 4)
                        pe.wait_ge(pair_taken, i + 1)
                        for a in range(2):
                            for t in range(TT):
                                ins = mm(ps[:, M[1], a:a + 1],
                                         disp[:, t, a, :, :].rearrange("p c s -> p (c s)").bitcast(F32),
                                         cpair[:, t, a:a + 1], start=t == 0, stop=t == TT - 1)
                        ins.then_inc(slots_gated, 1)
                pe.wait_ge(act_ready, i * 2 + 1)
                pe.wait_ge(outputs_ready, i * 2 + 1)
                down_unit(0, n_(8), PRE_U + 8)
                if not last:
                    pe.wait_ge(disp_ready, i + 2)
                    pe.wait_ge(dispT_ready, i + 1)
                    gather(0)
                    pe.wait_ge(gslot_ready, i + 1)
                    gather(1)
                down_unit(1, n_(9), PRE_U + 9)
                if not last:
                    pe.wait_ge(xT_ready, i * 4 + 6)
                turn_gu(i * 2 + 1)
                down_unit(2, n_(10), PRE_U + 10)
                if not last:
                    pe.wait_ge(gate_clipped, i * 2 + 2)
                    gather(2)
                    pe.wait_ge(up_clipped, i * 2 + 2)
                    gather(3)
                down_unit(3, n_(11), PRE_U + 11)
                gap = GU_U if last else 0
                if not last:
                    pe.wait_ge(gu_copied, i * 2 + 2)
                    pe.wait_ge(sel_ready, i * 2 + 3)
                    bias(0)
                    pe.wait_ge(xT_ready, i * 4 + 8)
                    for k in range(GU_U):
                        gu_unit(0, k, n_(12 + k), PRE_U + 12 + k)
                pe.wait_ge(act_ready, i * 2 + 2)
                pe.wait_ge(outputs_ready, i * 2 + 2)
                for u in range(DN_U):
                    down_unit(u, n_(20 + u - gap), PRE_U + 20 + u - gap)
                    if u == 1 and not last:
                        turn_gu(i * 2 + 2)

            with pe.Fori(0, last_pair) as i:
                iteration(i, False)
            iteration(last_pair, True)
            pe.wait_ge(outputs_ready, last_pair * 2 + 3)
            pe.wait_ge(gate_clipped, last_pair * 2 + 2)
            pe.wait_ge(up_clipped, last_pair * 2 + 2)
            scatter(0)
            scatter(1)
            pe.wait_ge(added, last_pair * 4 + TT + 5)
            scatter(2)
            pe.wait_ge(added, last_pair * 4 + TT + 6)
            scatter(3)


_INS = ["x", "g_mix", "w_in", "w_pool", "pool_scale", "w_out", "g_ffn", "w_router", "b_router",
        "w_gu", "b_gu", "w_down", "b_down", "g_final"]


def kernel(**inputs):
    import concourse.bacc as bacc
    from concourse.bass_utils import run_bass_kernel_spmd

    nc = bacc.Bacc("TRN2", target_bir_lowering=False, num_devices=1)
    arrays, args = {}, []
    for name in _INS + ["consts"]:
        a = np.ascontiguousarray(constants() if name == "consts" else inputs[name])
        arrays[f"in_{name}"] = a
        args.append(nc.dram_tensor(f"in_{name}", a.shape, mybir.dt.from_np(a.dtype), kind="ExternalInput").ap())
    args.append(nc.dram_tensor("out", (1, T, D), F32, kind="ExternalOutput").ap())
    hybrid_layer(nc, *args)
    r = run_bass_kernel_spmd(nc, [arrays], core_ids=[0])
    return r.results[0]["out"]
```

```python
from contextlib import ExitStack

import concourse.bass as bass
import numpy as np
from concourse import mybir

F32 = mybir.dt.float32
F32R = mybir.dt.float32r
I32 = mybir.dt.int32
U32 = mybir.dt.uint32
ALU = mybir.AluOpType
ACT = mybir.ActivationFunctionType
AX = mybir.AxisListType

P = 128
T, D = 256, 1024
TT = T // P
DC = D // P
DP = 512
DA = 512
H, HD = 8, 64
WINDOWS = (2, 4, 8, 16)
PATTERNS = ((128, 1), (512, 4), (2048, 16))
E, K, FE = 32, 4, 1024
LIMIT, ALPHA, EPS = 7.0, 1.702, 1e-5
NEG = -1e30
SLOTS = 64
PAD = 16
N_IN = DP + 3 * DA

UW = 2048
RAW = 8
SPL = 4
PLACE = (2, 3, 1, 0)
EARLY = 3
GU_U, DN_U = 8, 4
ITER_U = 2 * (GU_U + DN_U)
PRE_U = GU_U
PAIRS = E // 2

_AT, _n = {}, 0
for _name, _w in (("ident", P), ("earlier", P), ("ones", P), ("stack", SLOTS), ("slots", SLOTS), ("experts", E),
                  ("limits", 4), ("selsrc", E), ("count0", P), ("count1", 2 * P), ("invcount", 4 * PAD)):
    _AT[_name] = (_n, _n + _w)
    _n += _w
N_CONST = _n


def constants():
    c = np.zeros((P, N_CONST), np.float32)

    def put(name, a):
        lo, hi = _AT[name]
        c[:a.shape[0], lo:hi] = a

    r = np.arange(P)
    put("ident", np.eye(P))
    put("earlier", r[:, None] < r[None, :])
    put("ones", np.ones((P, P)))
    put("stack", np.concatenate([np.eye(SLOTS)] * 2))
    put("slots", np.tile(np.arange(SLOTS), (P, 1)))
    put("experts", np.tile(np.arange(E), (P, 1)))
    put("limits", np.tile([SLOTS, 2 * SLOTS, 3 * SLOTS, T], (P, 1)))
    put("selsrc", np.concatenate([np.eye(E)] * 4))
    diff = np.arange(T)[:, None] - np.arange(T)[None, :]
    seen = sum(((diff >= 0) & (diff % d == 0) & (diff // d <= w // d)).astype(np.float32) for w, d in PATTERNS)
    put("count0", seen[:P, :P])
    put("count1", seen[P:])
    put("invcount", np.tile(np.concatenate([1.0 / np.minimum(np.arange(PAD) + 1.0, w) for w in WINDOWS]), (P, 1)))
    return c


def hybrid_layer(nc, x, g_mix, w_in, w_pool, pool_scale, w_out, g_ffn, w_router, b_router,
                 w_gu, b_gu, w_down, b_down, g_final, consts, out):
    KB = 1024
    with ExitStack() as ctx:
        def sem(name):
            return ctx.enter_context(nc.semaphore(name))

        base = (nc.sbuf_base + 31) // 32 * 32
        arena_bytes = 207 * KB + 768
        ctx.enter_context(nc.sbuf_tensor("arena", [P, arena_bytes // 4], F32))

        def at(name, shape, dt, off):
            size = 4
            for s in shape[1:]:
                size *= s
            assert off + size <= arena_bytes, (name, off, size)
            return nc.alloc_sbuf_tensor_at(name, shape, dt, offset=base + off)

        raw = at("raw", [P, RAW, UW], F32, 0)
        split = at("split", [P, SPL, 2, UW], F32R, 64 * KB)
        gu = at("gu", [P, 2 * FE], F32, 128 * KB)
        gate = at("gate", [P, DC * SLOTS], F32, 136 * KB)
        sig = at("sig", [P, DC * SLOTS], F32, 138 * KB)
        lin = at("lin", [P, DC * SLOTS], F32, 140 * KB)
        actT = at("actT", [P, DC, 2, SLOTS], F32R, 142 * KB)
        ysc = at("ysc", [P, 2, D], F32, 146 * KB)
        disp = at("disp", [P, TT, 2, 2, SLOTS], F32R, 154 * KB)
        dispT = at("dispT", [P, 2, TT, P], F32, 156 * KB)
        h2h = at("h2h", [P, TT, D], F32R, 158 * KB)
        h2l = at("h2l", [P, TT, D], F32R, 166 * KB)
        acc = at("acc", [P, TT, D], F32, 174 * KB)
        bgu = at("bgu", [P, FE], F32R, 182 * KB)
        xT = at("xT", [P, 2, DC, 2, SLOTS], F32R, 190 * KB)
        outs = at("outs", [P, TT, D], F32, 0)
        junk3 = [at(f"junk3{t}", [P, D], F32, (8 + 4 * t) * KB) for t in range(TT)]
        gfin = at("gfin", [P, D], F32, 16 * KB)
        wout = at("wout", [P, DC, D], F32, 64 * KB)
        wsp = [at(f"wsp{n}", [P, 2, UW], F32R, off * KB) for n, off in enumerate((112, 158))]
        xr = at("xr", [P, TT, D], F32, 96 * KB)
        hTh = at("hTh", [P, DC, T], F32R, 104 * KB)
        hTl = at("hTl", [P, DC, T], F32R, 190 * KB)
        sm1 = at("sm1", [P, H, 2 * P], F32, 96 * KB)
        pr1 = at("pr1", [P, H, 2 * P], F32, 104 * KB)
        h2 = at("h2", [P, TT, D], F32, 64 * KB)
        h2T = at("h2T", [P, DC, T], F32, 72 * KB)
        junk = [at(f"junk{t}", [P, D], F32, (112 + 4 * t) * KB) for t in range(TT)]
        junk2 = [at(f"junk2{t}", [P, D], F32, (128 + 4 * t) * KB) for t in range(TT)]
        qT = at("qT", [P, 4, T], F32, 112 * KB)
        kT = at("kT", [P, 4, T], F32, 116 * KB)
        sm0 = at("sm0", [P, H, P], F32, 120 * KB)
        pr0 = at("pr0", [P, H, P], F32, 124 * KB)
        yat = at("yat", [P, TT, DA], F32, 120 * KB)
        W = PAD + T
        uT = at("uT", [P, 4, W], F32, 128 * KB)
        wsA = at("wsA", [P, 4, W], F32, 128 * KB + 16 * W)
        wsB = at("wsB", [P, 4, W], F32, 128 * KB + 32 * W)
        assert 48 * W <= 13 * KB
        wrt = at("wrt", [P, DC, E], F32, 141 * KB)
        wpool = at("wpool", [P, 4, P], F32, 142 * KB)
        vecs = at("vecs", [2 * DC + 4, P], F32, 144 * KB)
        gffn = at("gffn", [P, D], F32, 150 * KB)
        neg0 = at("neg0", [P, P], F32, 154 * KB)
        neg1 = at("neg1", [P, 2 * P], F32, 154 * KB + 512)
        prT = at("prT", [P, 3 * H, P], F32, 158 * KB)
        braw = at("braw", [P, FE], F32, 186 * KB)
        mixT = at("mixT", [P, DC, T], F32, 190 * KB)
        vau = at("vau", [P, TT, H, HD + 1], F32, 198 * KB)
        onehot = at("onehot", [P, TT, K, E], F32, 128 * KB)
        weighted = at("weighted", [P, TT, K, E], F32, 129 * KB)

        top = [0]

        def small(name, shape, dt=F32):
            size = 4
            for s in shape[1:]:
                size *= s
            top[0] += (size + 31) // 32 * 32
            return at(name, shape, dt, top[0] - (size + 31) // 32 * 32)

        top[0] = 198 * KB + 4 * TT * H * (HD + 1)
        cst = small("cst", [P, N_CONST])
        brt = small("brt", [P, E])
        vecT = small("vecT", [P, 2 * DC + 4])
        identr = small("identr", [P, P], F32R)
        ssq = small("ssq", [P, TT])
        inv = small("inv", [P, TT])
        rs = small("rs", [P, TT])
        mxs = small("mxs", [P, 2, H])
        nmx = small("nmx", [P, 2, H])
        rden = small("rden", [P, 2, H])
        scrap = small("scrap", [P, 1])
        top[0] = 198 * KB
        lg = small("lg", [P, TT, E])
        v8 = small("v8", [P, TT, 8])
        i8 = small("i8", [P, TT, 8], U32)
        i4 = small("i4", [P, TT, K])
        nv1 = small("nv1", [P, TT])
        e4 = small("e4", [P, TT, K])
        s4 = small("s4", [P, TT])
        r4 = small("r4", [P, TT])
        g4 = small("g4", [P, TT, K])
        mask = small("mask", [P, TT, E])
        comb = small("comb", [P, TT, E])
        rank1 = small("rank1", [P, TT, E])
        rank = small("rank", [P, TT, E])
        most = small("most", [P, 1])
        over = small("over", [P, 4])
        nover = small("nover", [P, 1])
        further = small("further", [P, 1], I32)
        cpair = small("cpair", [P, TT, 2])
        gslot = small("gslot", [P, 2])
        sel = small("sel", [P, 2, 2, SLOTS], F32R)
        assert top[0] <= 198 * KB + 4 * TT * H * (HD + 1)

        ps = ctx.enter_context(nc.psum_tensor("ps", [P, 8, 512], F32))
        GU, Y = 0, 4
        M = (6, 7)

        def c_(name, rows=P):
            lo, hi = _AT[name]
            return cst[0:rows, lo:hi]

        def bc(ap, *dims):
            return ap.broadcast_to(list(dims))

        x_loaded = [sem(f"x_loaded{t}") for t in range(TT)]
        raw_loaded = [sem(f"raw_loaded{s}") for s in range(RAW)]
        const_loaded, vec_loaded, wout_loaded = sem("const_loaded"), sem("vec_loaded"), sem("wout_loaded")
        wpool_loaded, router_loaded = sem("wpool_loaded"), sem("router_loaded")
        bgu_loaded, bdown_loaded = sem("bgu_loaded"), sem("bdown_loaded")
        gffn_loaded, gfin_loaded = sem("gffn_loaded"), sem("gfin_loaded")
        stored = sem("stored")
        squares, inv_ready, rstd_ready, scaled = sem("squares"), sem("inv_ready"), sem("rstd_ready"), sem("scaled")
        dve_step, pool_step = sem("dve_step"), sem("pool_step")
        vec_turned, vec_ready = sem("vec_turned"), sem("vec_ready")
        x_turned, hTh_ready, hTl_ready = sem("x_turned"), sem("hTh_ready"), sem("hTl_ready")
        win_high, win_low, ymix_dve = sem("win_high"), sem("win_low"), sem("ymix_dve")
        u_summed, qk_summed = sem("u_summed"), sem("qk_summed")
        win_used, q_ready, k_ready, u_ready, v_ready = (
            sem("win_used"), sem("q_ready"), sem("k_ready"), sem("u_ready"), sem("v_ready"))
        windows_summed, means_ready = sem("windows_summed"), sem("means_ready")
        pads_ready, pooled_ready, ypool_done, ypool_ready = (
            sem("pads_ready"), sem("pooled_ready"), sem("ypool_done"), sem("ypool_ready"))
        scores, masked, max_ready, exp_done, probs = (
            sem("scores"), sem("masked"), sem("max_ready"), sem("exp_done"), sem("probs"))
        probs_turned, prT_act, prT_dve, attended, yat_ready, yat_turned, ymix_ready = (
            sem("probs_turned"), sem("prT_act"), sem("prT_dve"), sem("attended"), sem("yat_ready"),
            sem("yat_turned"), sem("ymix_ready"))
        projected, h2_turned, h2T_act, h2T_dve, logits = (
            sem("projected"), sem("h2_turned"), sem("h2T_act"), sem("h2T_dve"), sem("logits"))
        h2h_ready, h2l_ready, bgu_high, bgu_ready, identr_ready = (
            sem("h2h_ready"), sem("h2l_ready"), sem("bgu_high"), sem("bgu_ready"), sem("identr_ready"))
        top_ready, exp4_done, mask_ready, ranked, comb_ready, comb_turned = (
            sem("top_ready"), sem("exp4_done"), sem("mask_ready"), sem("ranked"), sem("comb_ready"),
            sem("comb_turned"))
        combT_ready, rounds_ready, ysc_zeroed, dispT_zeroed = (
            sem("combT_ready"), sem("rounds_ready"), sem("ysc_zeroed"), sem("dispT_zeroed"))
        high_ready, low_ready, unit_used = sem("high_ready"), sem("low_ready"), sem("unit_used")
        sel_zeroed, sel_ready, bias_added = sem("sel_zeroed"), sem("sel_ready"), sem("bias_added")
        gu_copied, outputs_ready = sem("gu_copied"), sem("outputs_ready")
        gate_turned, up_turned, gate_clipped, up_clipped = (
            sem("gate_turned"), sem("up_turned"), sem("gate_clipped"), sem("up_clipped"))
        sig_done, gsig_done, act_done, act_high, act_ready = (
            sem("sig_done"), sem("gsig_done"), sem("act_done"), sem("act_high"), sem("act_ready"))
        disp_ready, gathered, xT_ready = sem("disp_ready"), sem("gathered"), sem("xT_ready")
        disp_turned, dispT_ready, slots_gated, gslot_ready = (
            sem("disp_turned"), sem("dispT_ready"), sem("slots_gated"), sem("gslot_ready"))
        scattered, added, pair_taken = sem("scattered"), sem("added"), sem("pair_taken")

        def pair_of(i):
            return i % PAIRS

        block = ctx.enter_context(nc.Block())

        @block.sync
        def _(sp):
            for t in range(TT):
                sp.dma_start(acc[:, t, :], x[0, t * P:(t + 1) * P, :]).then_inc(x_loaded[t], 16)
            sp.dma_start(cst[:], consts).then_inc(const_loaded, 16)
            for c in range(DC):
                sp.dma_start(raw[:, c, :], w_in[0, c * P:(c + 1) * P, :]).then_inc(raw_loaded[c], 16)
            sp.dma_start(wpool[:], w_pool[0].rearrange("g c d -> c g d")).then_inc(wpool_loaded, 16)
            for n in range(4):
                sp.dma_start(braw[n * E:(n + 1) * E, :], b_gu[0, :, n // 2 * FE:(n // 2 + 1) * FE]).then_inc(bgu_loaded, 16)
            sp.dma_start(wout[:], w_out[0].rearrange("(c p) n -> p c n", p=P)).then_inc(wout_loaded, 16)
            sp.dma_start(wrt[:], w_router[0].rearrange("(c p) e -> p c e", p=P)).then_inc(router_loaded, 16)
            sp.dma_start(brt[:], b_router.broadcast_to([P, E])).then_inc(router_loaded, 16)
            sp.dma_start(gffn[:], g_ffn.broadcast_to([P, D])).then_inc(gffn_loaded, 16)
            sp.wait_ge(ysc_zeroed, 1)
            sp.dma_start(ysc[0:E, 0, :], b_down[0]).then_inc(bdown_loaded, 16)

            def load(e, first, slot_unit):
                s = slot_unit % RAW
                if first < GU_U:
                    src = w_gu[0, bass.ds(e, 1), first * P:(first + 1) * P, :].rearrange("a p n -> p (a n)")
                    sp.dma_start(raw[:, s, :], src).then_inc(raw_loaded[s], 16)
                else:
                    u = first - GU_U
                    src = w_down[0, bass.ds(e, 1), 2 * u * P:2 * (u + 1) * P, :].rearrange(
                        "a (r p) n -> p (a r) n", p=P)
                    dst = raw[:, s, :].rearrange("p (r n) -> p r n", r=2)
                    sp.dma_start(dst, src).then_inc(raw_loaded[s], 16)

            for c in range(PRE_U):
                sp.wait_ge(win_low, c + 1)
                load(0, c, c)
            for k in range(EARLY):
                sp.wait_ge(low_ready, k + 1)
                load(1, k, k)
            sp.wait_ge(rounds_ready, 1)
            last_pair = sp.snap(sp.value_load(further[0:1, 0:1], min_val=0, max_val=T // SLOTS - 1) * PAIRS + (PAIRS - 1))

            def iteration(i, last):
                a = pair_of(i) * 2
                nxt = pair_of(i + 1) * 2
                for k in range(EARLY, ITER_U + (0 if last else EARLY)):
                    if last and k in range(GU_U + DN_U, 2 * GU_U + DN_U):
                        continue
                    at_ = k - (GU_U if last and k >= 2 * GU_U + DN_U else 0)
                    sp.wait_ge(low_ready, i * ITER_U + at_ + 1)
                    if k < GU_U:
                        load(a + 1, k, at_)
                    elif k < GU_U + DN_U:
                        load(a, k, at_)
                    elif k < 2 * GU_U + DN_U:
                        load(nxt, k - GU_U - DN_U, at_)
                    elif k < ITER_U:
                        load(a + 1, k - GU_U - DN_U, at_)
                    else:
                        load(nxt + 1, k - ITER_U, at_)

            with sp.Fori(0, last_pair) as i:
                iteration(i, False)
            iteration(last_pair, True)
            sp.wait_ge(low_ready, last_pair * ITER_U + PRE_U + 12)
            sp.dma_start(gfin[:], g_final.rearrange("(a n) -> a n", a=1).broadcast_to([P, D])).then_inc(gfin_loaded, 16)
            for t in range(TT):
                sp.wait_ge(scaled, 2 * TT + t + 1)
                sp.dma_start(out[0, t * P:(t + 1) * P, :], outs[:, t, :]).then_inc(stored, 16)
            sp.wait_ge(stored, 16 * TT)

        @block.gpsimd
        def _(pool):
            steps = [0]

            def link(ins):
                steps[0] += 1
                ins.then_inc(pool_step, 1)
                pool.wait_ge(pool_step, steps[0])

            pool.memset(uT[:, :, 0:PAD], 0.0).then_inc(pads_ready, 1)
            pool.memset(vau[:, :, :, HD:HD + 1], 1.0).then_inc(pads_ready, 1)
            pool.memset(ysc[:, 0, :], 0.0).then_inc(ysc_zeroed, 1)
            pool.wait_ge(const_loaded, 16)
            pool.wait_ge(u_ready, 1)
            pool.wait_ge(pads_ready, 2)
            link(pool.tensor_tensor(wsA[:, :, 1:W], uT[:, :, 1:W], uT[:, :, 0:W - 1], ALU.add))
            link(pool.tensor_tensor(wsB[:, 1:4, 3:W], wsA[:, 1:4, 3:W], wsA[:, 1:4, 1:W - 2], ALU.add))
            link(pool.tensor_tensor(wsA[:, 2:4, 7:W], wsB[:, 2:4, 7:W], wsB[:, 2:4, 3:W - 4], ALU.add))
            pool.tensor_tensor(wsB[:, 3:4, 15:W], wsA[:, 3:4, 15:W], wsA[:, 3:4, 7:W - 8], ALU.add).then_inc(windows_summed, 1)
            pool.wait_ge(windows_summed, 1)
            pool.wait_ge(win_used, DC)
            for g, w in enumerate(WINDOWS):
                ins = pool.tensor_tensor(mixT[:, 4 + g, 0:PAD], (wsA, wsB)[g % 2][:, g, PAD:2 * PAD],
                                         c_("invcount")[:, g * PAD:(g + 1) * PAD], ALU.mult)
            link(ins)
            pool.wait_ge(means_ready, 1)
            pool.tensor_tensor(mixT[:, 4:8, :], mixT[:, 4:8, :], uT[:, :, PAD:W], ALU.subtract).then_inc(pooled_ready, 1)
            pool.wait_ge(projected, 2)
            pool.memset(sel[:].bitcast(F32), 0.0).then_inc(sel_zeroed, 1)
            pool.memset(dispT[:], 0.0).then_inc(dispT_zeroed, 1)
            pool.wait_ge(scaled, 2 * TT)
            pool.memset(ysc[:, 1, :], 0.0).then_inc(ysc_zeroed, 1)
            def select(e, half):
                src = c_("selsrc")[:, bass.ds(e, 1)]
                pool.wait_ge(sel_zeroed, 1)
                pool.tensor_tensor(sel[:, half, 0, :], bc(src, P, SLOTS), c_("ones")[:, 0:SLOTS],
                                   ALU.mult).then_inc(sel_ready, 1)

            select(0, 0)
            pool.wait_ge(h2h_ready, 1)
            pool.tensor_tensor(h2l[:], h2[:], h2h[:].bitcast(F32), ALU.subtract).then_inc(h2l_ready, 1)
            pool.wait_ge(rounds_ready, 1)
            last_pair = pool.snap(pool.value_load(further[0:1, 0:1], min_val=0, max_val=T // SLOTS - 1) * PAIRS + (PAIRS - 1))

            with pool.Fori(0, last_pair) as i:
                pool.wait_ge(bias_added, i * 2 + 1)
                select(pair_of(i) * 2 + 1, 1)
                pool.wait_ge(bias_added, i * 2 + 1)
                select(pair_of(i + 1) * 2, 0)
            i = last_pair
            pool.wait_ge(bias_added, i * 2 + 1)
            select(pair_of(i) * 2 + 1, 1)

        @block.scalar
        def _(act):
            act.dma_start(vecs[0:DC, :], g_mix.rearrange("a (c p) -> (a c) p", p=P)).then_inc(vec_loaded, 16)
            act.dma_start(vecs[DC:DC + 4, :], pool_scale.rearrange("a (c p) -> (a c) p", p=P)).then_inc(vec_loaded, 16)
            act.dma_start(vecs[DC + 4:2 * DC + 4, :], g_ffn.rearrange("a (c p) -> (a c) p", p=P)).then_inc(vec_loaded, 16)

            def high(n, k, first_use):
                act.wait_ge(raw_loaded[k % RAW], (first_use + 1) * 16)
                if not isinstance(n, int) or n >= SPL:
                    act.wait_ge(unit_used, n - SPL + 1)
                act.activation(split[:, PLACE[k % SPL], 0, :], raw[:, k % RAW, :], ACT.Copy).then_inc(high_ready, 1)

            def norm(n, squares_of):
                for t in range(TT):
                    act.activation(squares_of[t][:], acc[:, t, :], ACT.Square, accum_out=ssq[:, t:t + 1]).then_inc(squares, 1)
                act.wait_ge(inv_ready, n + 1)
                act.activation(rs[:], inv[:], ACT.Sqrt).then_inc(rstd_ready, 1)

            act.wait_ge(const_loaded, 16)
            act.activation(scrap[:], c_("ones")[:, 0:1], ACT.Sqrt)
            for t in range(TT):
                act.wait_ge(x_loaded[t], 16)
            norm(0, junk)

            def win_part(c):
                act.wait_ge(raw_loaded[c], 16)
                if c >= 2:
                    act.wait_ge(win_used, c - 1)
                act.activation(wsp[c % 2][:, 0, :], raw[:, c, :], ACT.Copy).then_inc(win_high, 1)

            win_part(0)
            act.wait_ge(vec_ready, 1)
            for b in range(4):
                act.wait_ge(x_turned, b + 1)
                for c in (2 * b, 2 * b + 1):
                    ins = act.activation(hTh[:, c, :], ps[:, b, (c % 2) * T:(c % 2 + 1) * T], ACT.Copy,
                                         scale=vecT[:, c:c + 1])
                ins.then_inc(hTh_ready, 1)
            for c in range(1, DC):
                win_part(c)
                if c == 5:
                    act.wait_ge(bgu_loaded, 64)
                    act.activation(bgu[:], braw[:], ACT.Copy).then_inc(bgu_high, 1)
                    act.wait_ge(const_loaded, 16)
                    act.activation(identr[:], c_("ident"), ACT.Copy).then_inc(identr_ready, 1)
            act.wait_ge(u_summed, 1)
            act.activation(uT[:, :, PAD:W], ps[:, 4:6, :].rearrange("p a (b t) -> p (a b) t", b=2),
                           ACT.Copy).then_inc(u_ready, 1)
            act.wait_ge(qk_summed, 1)
            act.activation(qT[:].rearrange("p c t -> p (c t)"), ps[:, 0:2, :].rearrange("p a b -> p (a b)"),
                           ACT.Copy).then_inc(q_ready, 1)

            def exps(tile, pr, sm):
                act.wait_ge(max_ready, tile + 1)
                for s in range(H):
                    ins = act.activation(pr[:, s, :], sm[:, s, :], ACT.Exp, bias=nmx[:, tile, s:s + 1])
                ins.then_inc(exp_done, 1)

            act.wait_ge(windows_summed, 1)
            act.wait_ge(win_used, DC)
            for g, w in enumerate(WINDOWS):
                ins = act.activation(mixT[:, 4 + g, PAD:T], (wsA, wsB)[g % 2][:, g, 2 * PAD:W], ACT.Copy, scale=1.0 / w)
            ins.then_inc(means_ready, 1)
            exps(0, pr1, sm1)
            act.wait_ge(ypool_done, 1)
            for g in range(4):
                ins = act.activation(mixT[:, g, :], ps[:, 6 + g // 2, (g % 2) * T:(g % 2 + 1) * T], ACT.Copy,
                                     scale=vecT[:, DC + g:DC + g + 1])
            ins.then_inc(ypool_ready, 1)
            exps(1, pr0, sm0)
            for n in (0, 2, 4):
                act.wait_ge(probs_turned, n + 1)
                act.activation(prT[:, 4 * n:4 * n + 4, :].rearrange("p a b -> p (a b)"), ps[:, 4 + n % 4, :],
                               ACT.Copy).then_inc(prT_act, 1)
            act.wait_ge(yat_turned, 1)
            act.activation(mixT[:, 4:6, :].rearrange("p a b -> p (a b)"), ps[:, 6, :], ACT.Copy).then_inc(ymix_ready, 1)
            high(0, 0, 1)
            high(1, 1, 1)
            for t in range(TT):
                act.wait_ge(added, 1 + t)
                act.activation(junk2[t][:], acc[:, t, :], ACT.Square, accum_out=ssq[:, t:t + 1]).then_inc(squares, 1)
            for b in (1, 3):
                act.wait_ge(h2_turned, b + 1)
                for c in (2 * b, 2 * b + 1):
                    ins = act.activation(h2T[:, c, :], ps[:, b, (c % 2) * T:(c % 2 + 1) * T], ACT.Copy,
                                         scale=vecT[:, DC + 4 + c:DC + 5 + c])
                ins.then_inc(h2T_act, 1)
            act.wait_ge(inv_ready, 2)
            act.activation(rs[:], inv[:], ACT.Sqrt).then_inc(rstd_ready, 1)
            act.activation(scrap[:], c_("ones")[:, 0:1], ACT.Exp)
            act.wait_ge(scaled, 2 * TT)
            act.activation(h2h[:], h2[:], ACT.Copy).then_inc(h2h_ready, 1)
            act.wait_ge(top_ready, 1)
            for t in range(TT):
                act.activation(e4[:, t, :], v8[:, t, 0:K], ACT.Exp, bias=nv1[:, t:t + 1],
                               accum_out=s4[:, t:t + 1]).then_inc(exp4_done, 1)
            high(2, 2, 1)

            def gather_copy(job, count):
                act.wait_ge(gathered, count)
                act.activation(xT[:, :, 2 * job:2 * job + 2].rearrange("p e c a s -> p e (c a s)"),
                               ps[:, M[job % 2], :].rearrange("p (e n) -> p e n", e=2), ACT.Copy).then_inc(xT_ready, 1)

            def gu_copy(e, used):
                act.wait_ge(unit_used, used)
                if not isinstance(e, int):
                    act.wait_ge(up_turned, e)
                act.activation(gu[:], ps[:, 0:4, :].rearrange("p a b -> p (a b)"), ACT.Copy).then_inc(gu_copied, 1)

            def sigmoid(e):
                act.wait_ge(gate_clipped, e + 1)
                act.activation(sig[:], gate[:], ACT.Sigmoid, scale=ALPHA).then_inc(sig_done, 1)

            def act_split(e, used=None):
                act.wait_ge(act_done, e + 1)
                if used is not None:
                    act.wait_ge(unit_used, used)
                act.activation(actT[:, :, 0, :], lin[:].rearrange("p (c s) -> p c s", s=SLOTS),
                               ACT.Copy).then_inc(act_high, 1)

            def y_copy(i, half, used):
                act.wait_ge(unit_used, used)
                act.wait_ge(gslot_ready, i + 1)
                act.wait_ge(scattered, i * 4 + 4)
                act.activation(ysc[:, half, :], ps[:, Y:Y + 2, :].rearrange("p a b -> p (a b)"), ACT.Copy,
                               scale=gslot[:, half:half + 1]).then_inc(outputs_ready, 1)

            act.wait_ge(h2l_ready, 1)
            high(3, 3, 1)
            act.wait_ge(rounds_ready, 1)
            last_pair = act.snap(act.value_load(further[0:1, 0:1], min_val=0, max_val=T // SLOTS - 1) * PAIRS + (PAIRS - 1))
            for job in range(4):
                gather_copy(job, job + 1)
            for k in range(SPL, PRE_U):
                high(k, k, 1)
            gu_copy(0, PRE_U)

            def unit(i, k, skipped=0):
                k -= skipped
                high(i * ITER_U + PRE_U + k, PRE_U + k, i * (ITER_U // RAW) + 2 + k // RAW)

            unit(0, 0)
            unit(0, 1)
            sigmoid(0)

            def used(i, k):
                return i * ITER_U + (PRE_U + k)

            def iteration(i, last):
                unit(i, 2)
                unit(i, 3)
                unit(i, 4)
                act_split(i * 2)
                for k in range(5, 10):
                    unit(i, k)
                gu_copy(i * 2 + 1, used(i, GU_U))
                unit(i, 10)
                if not last:
                    gather_copy(0, i * 4 + 5)
                    gather_copy(1, i * 4 + 6)
                unit(i, 11)
                if not last:
                    unit(i, 12)
                    unit(i, 13)
                    sigmoid(i * 2 + 1)
                    y_copy(i, 0, used(i, 12))
                    gather_copy(2, i * 4 + 7)
                    gather_copy(3, i * 4 + 8)
                    for k in range(14, 18):
                        unit(i, k)
                    act_split(i * 2 + 1, used(i, 12))
                    for k in range(18, 22):
                        unit(i, k)
                    gu_copy(i * 2 + 2, used(i, 20))
                    unit(i, 22)
                    unit(i, 23)
                    unit(i, 24)
                    unit(i, 25)
                    sigmoid(i * 2 + 2)
                else:
                    sigmoid(i * 2 + 1)
                    act.wait_ge(rstd_ready, 2)
                    act.activation(scrap[:], rs[:, 0:1], ACT.Sqrt)
                    unit(i, 20, GU_U)
                    y_copy(i, 0, used(i, 12))
                    act_split(i * 2 + 1, used(i, 12))
                    for k in range(21, 24):
                        unit(i, k, GU_U)
                y_copy(i, 1, used(i, 24 - (GU_U if last else 0)))

            with act.Fori(0, last_pair) as i:
                iteration(i, False)
            iteration(last_pair, True)
            for t in range(TT):
                act.wait_ge(added, last_pair * 4 + 6 + TT + 2 * t)
                act.activation(junk3[t][:], acc[:, t, :], ACT.Square, accum_out=ssq[:, t:t + 1]).then_inc(squares, 1)
            act.wait_ge(inv_ready, 3)
            act.activation(rs[:], inv[:], ACT.Sqrt).then_inc(rstd_ready, 1)

        @block.vector
        def _(dve):
            steps = [0]

            def link(ins):
                steps[0] += 1
                ins.then_inc(dve_step, 1)
                dve.wait_ge(dve_step, steps[0])

            def inverse(n):
                dve.wait_ge(squares, 2 * n + 2)
                link(dve.tensor_scalar(inv[:], ssq[:], 1.0 / D, EPS, ALU.mult, ALU.add))
                dve.reciprocal(inv[:], inv[:]).then_inc(inv_ready, 1)
                dve.wait_ge(rstd_ready, n + 1)

            def low(n, k):
                dve.wait_ge(high_ready, n + 1)
                dve.tensor_tensor(split[:, PLACE[k % SPL], 1, :], raw[:, k % RAW, :], split[:, PLACE[k % SPL], 0, :].bitcast(F32),
                                  ALU.subtract).then_inc(low_ready, 1)

            dve.wait_ge(const_loaded, 16)
            dve.tensor_scalar(neg0[:], c_("count0"), 0.0, NEG, ALU.is_equal, ALU.mult)
            link(dve.tensor_scalar(neg1[:], c_("count1"), 0.0, NEG, ALU.is_equal, ALU.mult))
            inverse(0)
            for t in range(TT):
                dve.tensor_scalar(xr[:, t, :], acc[:, t, :], rs[:, t:t + 1], None, ALU.mult).then_inc(scaled, 1)
            dve.wait_ge(vec_turned, 1)
            dve.tensor_copy(vecT[:], ps[:, 7, 0:2 * DC + 4]).then_inc(vec_ready, 1)
            dve.wait_ge(vec_ready, 1)

            def win_rest(c):
                dve.wait_ge(win_high, c + 1)
                dve.tensor_tensor(wsp[c % 2][:, 1, :], raw[:, c, :], wsp[c % 2][:, 0, :].bitcast(F32),
                                  ALU.subtract).then_inc(win_low, 1)

            win_rest(0)
            for b in range(4):
                dve.wait_ge(hTh_ready, b + 1)
                for c in (2 * b, 2 * b + 1):
                    ins = dve.scalar_tensor_tensor(
                        out=hTl[:, c, :], in0=ps[:, b, (c % 2) * T:(c % 2 + 1) * T], scalar=vecT[:, c:c + 1],
                        in1=hTh[:, c, :].bitcast(F32), op0=ALU.mult, op1=ALU.subtract)
                ins.then_inc(hTl_ready, 1)
            for c in range(1, DC):
                win_rest(c)
                if c == 6:
                    dve.wait_ge(bgu_high, 1)
                    for r in (E, 3 * E):
                        ins = dve.tensor_tensor(bgu[r:r + E, :], braw[r:r + E, :], bgu[r:r + E, :].bitcast(F32),
                                                ALU.subtract)
                    ins.then_inc(bgu_ready, 1)
            dve.wait_ge(qk_summed, 1)
            dve.tensor_copy(kT[:].rearrange("p c t -> p (c t)"),
                            ps[:, 2:4, :].rearrange("p a b -> p (a b)")).then_inc(k_ready, 1)
            dve.wait_ge(win_used, DC)
            for t in range(TT):
                ins = dve.tensor_copy(vau[:, t, :, 0:HD], ps[:, 6 + t, :].rearrange("p (h d) -> p h d", h=H))
            ins.then_inc(v_ready, 1)

            def mask_and_max(n, sm, bank, neg, keys):
                dve.wait_ge(scores, n + 1)
                dve.scalar_tensor_tensor(
                    out=sm[:], in0=ps[:, bank:bank + H * keys // 512, :].rearrange("p a (b k) -> p (a b) k", k=keys),
                    scalar=HD ** -0.5, in1=bc(neg[:].rearrange("p (a k) -> p a k", a=1), P, H, keys),
                    op0=ALU.mult, op1=ALU.add).then_inc(masked, 1)
                dve.wait_ge(masked, n + 1)
                link(dve.tensor_reduce(mxs[:, n, :], sm[:], AX.X, ALU.max))
                dve.tensor_scalar(nmx[:, n, :], mxs[:, n, :], -1.0, None, ALU.mult).then_inc(max_ready, 1)

            def times_count(n, pr, count, keys):
                dve.wait_ge(exp_done, n + 1)
                dve.tensor_tensor(pr[:], pr[:], bc(c_(count).rearrange("p (a k) -> p a k", a=1), P, H, keys),
                                  ALU.mult).then_inc(probs, 1)

            mask_and_max(0, sm1, 0, neg1, 2 * P)
            mask_and_max(1, sm0, 4, neg0, P)
            times_count(0, pr1, "count1", 2 * P)
            times_count(1, pr0, "count0", P)
            for n in (1, 3, 5):
                dve.wait_ge(probs_turned, n + 1)
                dve.tensor_copy(prT[:, 4 * n:4 * n + 4, :].rearrange("p a b -> p (a b)"),
                                ps[:, 4 + n % 4, :]).then_inc(prT_dve, 1)
            for n in range(2):
                dve.wait_ge(attended, n + 1)
                o = ps[:, 6 - 2 * n:8 - 2 * n, 0:4 * (HD + 1)].rearrange("p a (h d) -> p a h d", d=HD + 1)
                link(dve.reciprocal(rden[:, n, :].rearrange("p (a h) -> p a h", a=2), o[:, :, :, HD]))
                for half in range(2):
                    r = rden[:, n, 4 * half:4 * half + 4].rearrange("p (h a) -> p h a", a=1)
                    ins = dve.tensor_tensor(
                        yat[:, 1 - n, half * 256:half * 256 + 256].rearrange("p (h d) -> p h d", d=HD),
                        o[:, half, :, 0:HD], bc(r, P, 4, HD), ALU.mult)
                ins.then_inc(yat_ready, 1)
            dve.wait_ge(yat_turned, 1)
            dve.tensor_copy(mixT[:, 6:8, :].rearrange("p a b -> p (a b)"), ps[:, 7, :]).then_inc(ymix_dve, 1)
            low(0, 0)
            low(1, 1)
            for t in range(TT):
                dve.wait_ge(projected, t + 1)
                dve.tensor_tensor(acc[:, t, :], ps[:, 2 * t:2 * t + 2, :].rearrange("p a b -> p (a b)"),
                                  acc[:, t, :], ALU.add).then_inc(added, 1)
            for b in (0, 2):
                dve.wait_ge(h2_turned, b + 1)
                for c in (2 * b, 2 * b + 1):
                    ins = dve.tensor_scalar(h2T[:, c, :], ps[:, b, (c % 2) * T:(c % 2 + 1) * T],
                                            vecT[:, DC + 4 + c:DC + 5 + c], None, ALU.mult)
                ins.then_inc(h2T_dve, 1)
            dve.wait_ge(squares, 4)
            link(dve.tensor_scalar(inv[:], ssq[:], 1.0 / D, EPS, ALU.mult, ALU.add))
            dve.reciprocal(inv[:], inv[:]).then_inc(inv_ready, 1)
            dve.wait_ge(rstd_ready, 2)
            dve.wait_ge(gffn_loaded, 16)
            for t in range(TT):
                dve.scalar_tensor_tensor(out=h2[:, t, :], in0=acc[:, t, :], scalar=rs[:, t:t + 1], in1=gffn[:],
                                         op0=ALU.mult, op1=ALU.mult).then_inc(scaled, 1)
            dve.wait_ge(logits, 1)
            dve.wait_ge(router_loaded, 32)
            for t in range(TT):
                link(dve.scalar_tensor_tensor(out=lg[:, t, :], in0=ps[:, 4, t * E:(t + 1) * E], scalar=rs[:, t:t + 1],
                                              in1=brt[:], op0=ALU.mult, op1=ALU.add))
            for t in range(TT):
                link(dve.max(v8[:, t, :], lg[:, t, :]))
                link(dve.max_index(i8[:, t, :], v8[:, t, :], lg[:, t, :]))
            dve.tensor_scalar(nv1[:], v8[:, :, 0], -1.0, None, ALU.mult).then_inc(top_ready, 1)
            link(dve.tensor_copy(i4[:], i8[:, :, 0:K]))
            link(dve.tensor_tensor(onehot[:].rearrange("p t k e -> p (t k) e"),
                                   bc(c_("experts").rearrange("p (a e) -> p a e", a=1), P, TT * K, E),
                                   bc(i4[:].rearrange("p t (k a) -> p (t k) a", a=1), P, TT * K, E), ALU.is_equal))
            dve.tensor_reduce(mask[:], onehot[:].rearrange("p t k e -> p t e k"), AX.X, ALU.add).then_inc(mask_ready, 1)
            dve.wait_ge(exp4_done, 2)
            link(dve.reciprocal(r4[:], s4[:]))
            link(dve.tensor_tensor(g4[:], e4[:], bc(r4[:].rearrange("p (t a) -> p t a", a=1), P, TT, K), ALU.mult))
            link(dve.tensor_tensor(weighted[:].rearrange("p t k e -> p (t k) e"),
                                   onehot[:].rearrange("p t k e -> p (t k) e"),
                                   bc(g4[:].rearrange("p t (k a) -> p (t k) a", a=1), P, TT * K, E), ALU.mult))
            dve.tensor_reduce(comb[:], weighted[:].rearrange("p t k e -> p t e k"), AX.X, ALU.add).then_inc(comb_ready, 1)
            dve.wait_ge(ranked, 1)
            dve.wait_ge(mask_ready, 1)
            link(dve.scalar_tensor_tensor(out=rank1[:], in0=ps[:, 5, 0:TT * E].rearrange("p (t e) -> p t e", t=TT),
                                          scalar=1.0, in1=mask[:], op0=ALU.add, op1=ALU.mult))
            link(dve.tensor_scalar(rank[:], rank1[:], -1.0, None, ALU.add))
            link(dve.tensor_reduce(most[:], ps[:, 5, TT * E:TT * E + E], AX.X, ALU.max))
            link(dve.tensor_scalar(over[:], c_("limits"), most[:, 0:1], None, ALU.is_lt))
            link(dve.tensor_reduce(nover[:], over[:], AX.X, ALU.add))
            dve.tensor_copy(further[:], nover[:]).then_inc(rounds_ready, 1)

            def build_disp(e):
                for t in range(TT):
                    mine = rank[:, t, bass.ds(e, 2)].rearrange("p (a b) -> p a b", b=1)
                    for copy in range(2):
                        ins = dve.tensor_tensor(disp[:, t, :, copy, :],
                                                bc(c_("slots").rearrange("p (a s) -> p a s", a=1), P, 2, SLOTS),
                                                bc(mine, P, 2, SLOTS), ALU.is_equal)
                ins.then_inc(disp_ready, 1)

            def next_round(e, count):
                dve.tensor_copy(cpair[:], comb[:, :, bass.ds(e, 2)])
                dve.wait_ge(disp_ready, count)
                dve.tensor_scalar(rank[:, :, bass.ds(e, 2)], rank[:, :, bass.ds(e, 2)], -float(SLOTS), None,
                                  ALU.add).then_inc(pair_taken, 1)

            dve.wait_ge(comb_ready, 1)
            build_disp(0)
            next_round(0, 1)
            low(2, 2)
            dve.wait_ge(rounds_ready, 1)
            last_pair = dve.snap(dve.value_load(further[0:1, 0:1], min_val=0, max_val=T // SLOTS - 1) * PAIRS + (PAIRS - 1))
            dve.wait_ge(comb_turned, 1)
            dve.wait_ge(dispT_zeroed, 1)
            dve.tensor_copy(dispT[0:E, 0, :, :], ps[0:E, 4, 0:T].rearrange("p (t q) -> p t q", t=TT)).then_inc(outputs_ready, 1)

            def clip(e):
                dve.wait_ge(gate_turned, e + 1)
                dve.tensor_scalar(gate[:], ps[:, M[0], :], LIMIT, None, ALU.min).then_inc(gate_clipped, 1)
                dve.wait_ge(up_turned, e + 1)
                dve.tensor_scalar(lin[:], ps[:, M[1], :], -LIMIT, LIMIT, ALU.max, ALU.min).then_inc(up_clipped, 1)

            def swiglu(e):
                dve.wait_ge(sig_done, e + 1)
                dve.tensor_tensor(sig[:], gate[:], sig[:], ALU.mult).then_inc(gsig_done, 1)
                dve.wait_ge(gsig_done, e + 1)
                dve.scalar_tensor_tensor(out=lin[:], in0=lin[:], scalar=1.0, in1=sig[:], op0=ALU.add,
                                         op1=ALU.mult).then_inc(act_done, 1)

            def act_low(e):
                dve.wait_ge(act_high, e + 1)
                dve.tensor_tensor(actT[:, :, 1, :], lin[:].rearrange("p (c s) -> p c s", s=SLOTS),
                                  actT[:, :, 0, :].bitcast(F32), ALU.subtract).then_inc(act_ready, 1)

            def add_scattered(i, job):
                dve.wait_ge(scattered, i * 4 + job + 1)
                part = acc[:, job // 2, (job % 2) * 512:(job % 2 + 1) * 512]
                dve.tensor_tensor(part, ps[:, M[job % 2], :], part, ALU.add).then_inc(added, 1)

            for k in range(3, PRE_U):
                low(k, k)
            clip(0)

            def iteration(i, last):
                def unit(k, skipped=0):
                    low(i * ITER_U + (PRE_U + k - skipped), PRE_U + k - skipped)

                unit(0)
                unit(1)
                swiglu(i * 2)
                unit(2)
                unit(3)
                act_low(i * 2)
                add_scattered(i, 0)
                add_scattered(i, 1)
                unit(4)
                add_scattered(i, 2)
                add_scattered(i, 3)
                unit(5)
                unit(6)
                dve.wait_ge(disp_turned, i + 1)
                dve.tensor_copy(dispT[:].rearrange("p a t q -> p (a t q)"), ps[:, M[0], :]).then_inc(dispT_ready, 1)
                unit(7)
                dve.wait_ge(slots_gated, i + 1)
                dve.tensor_copy(gslot[:], ps[:, M[1], 0:2]).then_inc(gslot_ready, 1)
                if not last:
                    dve.wait_ge(pair_taken, i + 1)
                    e = dve.snap(pair_of(i + 1) * 2)
                    build_disp(e)
                    next_round(e, i + 2)
                unit(8)
                unit(9)
                unit(10)
                unit(11)
                clip(i * 2 + 1)
                if not last:
                    unit(12)
                    unit(13)
                    unit(14)
                    swiglu(i * 2 + 1)
                    unit(15)
                    unit(16)
                    act_low(i * 2 + 1)
                    for k in range(17, 24):
                        unit(k)
                    clip(i * 2 + 2)
                else:
                    swiglu(i * 2 + 1)
                    unit(20, GU_U)
                    act_low(i * 2 + 1)
                    for k in range(21, 24):
                        unit(k, GU_U)

            with dve.Fori(0, last_pair) as i:
                iteration(i, False)
            iteration(last_pair, True)
            for job in range(4):
                dve.wait_ge(scattered, last_pair * 4 + job + 5)
                part = acc[:, job // 2, (job % 2) * 512:(job % 2 + 1) * 512]
                dve.tensor_tensor(part, ps[:, job, :], part, ALU.add).then_inc(added, 1)
            inverse(2)
            dve.wait_ge(gfin_loaded, 16)
            for t in range(TT):
                dve.scalar_tensor_tensor(out=outs[:, t, :], in0=acc[:, t, :], scalar=rs[:, t:t + 1], in1=gfin[:],
                                         op0=ALU.mult, op1=ALU.mult).then_inc(scaled, 1)

        @block.tensor
        def _(pe):
            def mm(out_, lhsT, rhs, start=True, stop=True, shared=False):
                return pe.matmul(out_, lhsT, rhs, start=start, stop=stop, skip_group_check=shared)

            pe.wait_ge(const_loaded, 16)
            pe.wait_ge(vec_loaded, 48)
            pe.transpose(ps[:, 7, 0:2 * DC + 4], vecs[:], c_("ident", 2 * DC + 4)[:, 0:2 * DC + 4]).then_inc(vec_turned, 1)

            def turn(src, done):
                for c in range(DC):
                    for t in range(TT):
                        ins = pe.transpose(ps[:, c // 2, (c % 2) * T + t * P:(c % 2) * T + (t + 1) * P],
                                           src[:, t, c * P:(c + 1) * P], c_("ident"))
                    if c % 2:
                        ins.then_inc(done, 1)

            pe.wait_ge(scaled, 2)
            turn(xr, x_turned)
            def by_channel(c, bank, column):
                wh, wl = wsp[c % 2][:, 0, :], wsp[c % 2][:, 1, :]
                first, last = c == 0, c == DC - 1
                for j in range(4):
                    o = ps[:, bank + j // 2, (j % 2) * T:(j % 2 + 1) * T]
                    cols = slice(column + j * P, column + (j + 1) * P)
                    mm(o, wh[:, cols], hTh[:, c, :], start=first and j % 2 == 0, stop=False, shared=True)
                    mm(o, wh[:, cols], hTl[:, c, :], start=False, stop=False, shared=True)
                    ins = mm(o, wl[:, cols], hTh[:, c, :], start=False, stop=last, shared=True)
                return ins

            def by_token(c):
                wh, wl = wsp[c % 2][:, 0, :], wsp[c % 2][:, 1, :]
                first, last = c == 0, c == DC - 1
                for t in range(TT):
                    o, cols, tok = ps[:, 6 + t, :], slice(DP + 2 * DA, N_IN), slice(t * P, (t + 1) * P)
                    mm(o, hTh[:, c, tok], wh[:, cols], start=first, stop=False)
                    mm(o, hTh[:, c, tok], wl[:, cols], start=False, stop=False)
                    ins = mm(o, hTl[:, c, tok], wh[:, cols], start=False, stop=last)
                return ins

            for c in range(DC):
                if c < 2:
                    pe.wait_ge(hTl_ready, 1)
                pe.wait_ge(win_low, c + 1)
                u = by_channel(c, 4, 0)
                if c == 0:
                    pe.wait_ge(vec_ready, 1)
                    by_token(c)
                    pe.wait_ge(hTl_ready, 4)
                by_channel(c, 0, DP)
                qk = by_channel(c, 2, DP + DA)
                if c == DC - 1:
                    u.then_inc(u_summed, 1)
                    qk.then_inc(qk_summed, 1)
                (by_token(c) if c else qk).then_inc(win_used, 1)
            pe.wait_ge(q_ready, 1)
            pe.wait_ge(k_ready, 1)
            for n, (bank, keys) in enumerate(((0, 2 * P), (4, P))):
                if n == 1:
                    pe.wait_ge(u_ready, 1)
                tile = 1 - n
                for h in range(H):
                    s = (h % 2) * 4 + h // 2
                    rows = slice((h % 2) * HD, (h % 2 + 1) * HD)
                    per = 512 // keys
                    ins = mm(ps[:, bank + s // per, (s % per) * keys:(s % per + 1) * keys],
                             qT[rows, h // 2, tile * P:(tile + 1) * P], kT[rows, h // 2, 0:keys])
                ins.then_inc(scores, 1)
            pe.wait_ge(pooled_ready, 1)
            pe.wait_ge(wpool_loaded, 16)
            pe.wait_ge(v_ready, 1)
            for g in range(4):
                ins = mm(ps[:, 6 + g // 2, (g % 2) * T:(g % 2 + 1) * T], wpool[:, g, :], mixT[:, 4 + g, :])
            ins.then_inc(ypool_done, 1)
            def project(t, n, chunks):
                for c in chunks:
                    ins = mm(ps[:, 2 * t + n, :], mixT[:, c, t * P:(t + 1) * P],
                             wout[:, c, n * 512:(n + 1) * 512], start=c == 0, stop=c == DC - 1)
                return ins

            pe.wait_ge(ypool_ready, 1)
            pe.wait_ge(wout_loaded, 16)
            pe.wait_ge(masked, 1)
            project(0, 0, range(4))
            project(0, 1, range(4))
            pe.wait_ge(probs, 1)
            pe.wait_ge(masked, 2)
            for n in range(6):
                if n == 4:
                    project(1, 0, range(2))
                    pe.wait_ge(probs, 2)
                    pe.wait_ge(prT_act, 1)
                if n == 5:
                    pe.wait_ge(prT_dve, 1)
                for j in range(4):
                    src = pr0[:, 4 * (n - 4) + j, :] if n >= 4 else pr1[:, 2 * n + j // 2, (j % 2) * P:(j % 2 + 1) * P]
                    ins = pe.transpose(ps[:, 4 + n % 4, j * P:(j + 1) * P], src, c_("ident"))
                ins.then_inc(probs_turned, 1)

            def attend(tile, bank):
                for h in range(H):
                    s = (h % 2) * 4 + h // 2
                    out_ = ps[:, bank + h // 4, (h % 4) * (HD + 1):(h % 4 + 1) * (HD + 1)]
                    for kb in range(tile + 1):
                        src = 2 * s + kb if tile else 2 * H + s
                        ins = mm(out_, prT[:, src, :], vau[:, kb, h, :], start=kb == 0, stop=kb == tile)
                ins.then_inc(attended, 1)

            project(1, 0, range(2, 4))
            pe.wait_ge(prT_act, 2)
            pe.wait_ge(prT_dve, 2)
            pe.wait_ge(pads_ready, 2)
            attend(1, 6)
            pe.wait_ge(prT_act, 3)
            pe.wait_ge(prT_dve, 3)
            attend(0, 4)
            project(1, 1, range(2))
            pe.wait_ge(yat_ready, 2)
            for j in range(4):
                for t in range(TT):
                    ins = pe.transpose(ps[:, 6 + j // 2, (j % 2) * T + t * P:(j % 2) * T + (t + 1) * P],
                                       yat[:, t, j * P:(j + 1) * P], c_("ident"))
            ins.then_inc(yat_turned, 1)
            project(1, 1, range(2, 4))
            pe.wait_ge(ymix_ready, 1)
            pe.wait_ge(ymix_dve, 1)
            for t in range(TT):
                project(t, 0, range(4, DC))
                project(t, 1, range(4, DC)).then_inc(projected, 1)
            pe.wait_ge(added, TT)
            turn(acc, h2_turned)
            pe.wait_ge(router_loaded, 32)
            for c in range(DC):
                pe.wait_ge((h2T_dve, h2T_act)[c // 2 % 2], c // 4 + 1)
                for t in range(TT):
                    ins = mm(ps[:, 4, t * E:(t + 1) * E], h2T[:, c, t * P:(t + 1) * P], wrt[:, c, :],
                             start=c == 0 and t == 0, stop=c == DC - 1, shared=True)
            ins.then_inc(logits, 1)
            pe.wait_ge(mask_ready, 1)
            mm(ps[:, 5, 0:E], c_("earlier"), mask[:, 0, :])
            mm(ps[:, 5, E:2 * E], c_("ones"), mask[:, 0, :], stop=False)
            mm(ps[:, 5, E:2 * E], c_("earlier"), mask[:, 1, :], start=False)
            mm(ps[:, 5, 2 * E:3 * E], c_("ones"), mask[:, 0, :], stop=False)
            mm(ps[:, 5, 2 * E:3 * E], c_("ones"), mask[:, 1, :], start=False).then_inc(ranked, 1)
            pe.wait_ge(comb_ready, 1)
            for t in range(TT):
                ins = pe.transpose(ps[0:E, 4, t * P:(t + 1) * P], comb[:, t, :], c_("ident"))
            ins.then_inc(comb_turned, 1)

            def gather(job):
                bank = ps[:, M[job % 2], :].rearrange("p (e c a s) -> p c a e s", e=2, c=2, a=2)
                for c in (2 * job, 2 * job + 1):
                    for part, src in enumerate((h2h, h2l)):
                        for t in range(TT):
                            ins = mm(bank[:, c % 2, part], src[:, t, c * P:(c + 1) * P],
                                     disp[:, t, :, 0, :], start=t == 0, stop=t == TT - 1)
                ins.then_inc(gathered, 1)

            def bias(half):
                for n in range(4):
                    rows = slice(n // 2 * 2 * E, (n // 2 + 1) * 2 * E)
                    ins = mm(ps[:, GU + n, :], sel[rows, half, :, :].rearrange("p a s -> p (a s)"),
                             bgu[rows, (n % 2) * 512:(n % 2 + 1) * 512], stop=False)
                ins.then_inc(bias_added, 1)

            def gu_unit(half, c, n, k):
                pe.wait_ge(low_ready, n + 1)
                for b in range(4):
                    for part in range(2):
                        ins = mm(ps[:, GU + b, :], xT[:, half, c].rearrange("p a s -> p (a s)"), split[:, PLACE[k % SPL], part, b * 512:(b + 1) * 512],
                                 start=False, stop=c == GU_U - 1 and part == 1)
                ins.then_inc(unit_used, 1)

            def down_unit(u, n, k):
                pe.wait_ge(low_ready, n + 1)
                for r in range(2):
                    m = 2 * u + r
                    for b in range(2):
                        for part in range(2):
                            col = r * D + b * 512
                            ins = mm(ps[:, Y + b, :], actT[:, m, :, :].rearrange("p a s -> p (a s)"),
                                     split[:, PLACE[k % SPL], part, col:col + 512],
                                     start=m == 0 and part == 0, stop=m == DC - 1 and part == 1)
                ins.then_inc(unit_used, 1)

            def turn_gu(e):
                pe.wait_ge(gu_copied, e + 1)
                for b, done in enumerate((gate_turned, up_turned)):
                    for m in range(DC):
                        ins = mm(ps[:, M[b], m * SLOTS:(m + 1) * SLOTS],
                                 gu[:, b * FE + m * P:b * FE + (m + 1) * P], c_("stack"))
                    ins.then_inc(done, 1)

            def scatter(job):
                t, n = job // 2, job % 2
                for a in range(2):
                    ins = mm(ps[:, M[job % 2], :], dispT[:, a, t, :], ysc[:, a, n * 512:(n + 1) * 512],
                             start=a == 0, stop=a == 1)
                ins.then_inc(scattered, 1)

            pe.wait_ge(sel_ready, 1)
            pe.wait_ge(bgu_ready, 1)
            bias(0)
            pe.wait_ge(rounds_ready, 1)
            last_pair = pe.snap(pe.value_load(further[0:1, 0:1], min_val=0, max_val=T // SLOTS - 1) * PAIRS + (PAIRS - 1))
            pe.wait_ge(disp_ready, 1)
            pe.wait_ge(h2h_ready, 1)
            pe.wait_ge(h2l_ready, 1)
            for job in range(4):
                if job >= 2:
                    pe.wait_ge(xT_ready, job - 1)
                gather(job)
            pe.wait_ge(xT_ready, 4)
            for c in range(GU_U):
                gu_unit(0, c, c, c)
            pe.wait_ge(bdown_loaded, 16)
            pe.wait_ge(ysc_zeroed, 2)
            pe.wait_ge(identr_ready, 1)
            turn_gu(0)

            def iteration(i, last):
                def n_(k):
                    return i * ITER_U + PRE_U + k

                pe.wait_ge(gu_copied, i * 2 + 1)
                pe.wait_ge(sel_ready, i * 2 + 2)
                bias(1)
                for k in range(GU_U):
                    gu_unit(1, k, n_(k), PRE_U + k)
                    if k == 1:
                        pe.wait_ge(outputs_ready, i * 2 + 1)
                        pe.wait_ge(gate_clipped, i * 2 + 1)
                        scatter(0)
                        pe.wait_ge(up_clipped, i * 2 + 1)
                        scatter(1)
                    if k == 2:
                        pe.wait_ge(added, i * 4 + TT + 1)
                        scatter(2)
                        pe.wait_ge(added, i * 4 + TT + 2)
                        scatter(3)
                    if k == 3:
                        pe.wait_ge(added, i * 4 + TT + 3)
                        for a in range(2):
                            for t in range(TT):
                                ins = mm(ps[:, M[0], (2 * a + t) * P:(2 * a + t + 1) * P],
                                         disp[:, t, a, :, :].rearrange("p c s -> p (c s)"), identr[:])
                        ins.then_inc(disp_turned, 1)
                    if k == 4:
                        pe.wait_ge(added, i * 4 + TT + 4)
                        pe.wait_ge(pair_taken, i + 1)
                        for a in range(2):
                            for t in range(TT):
                                ins = mm(ps[:, M[1], a:a + 1],
                                         disp[:, t, a, :, :].rearrange("p c s -> p (c s)").bitcast(F32),
                                         cpair[:, t, a:a + 1], start=t == 0, stop=t == TT - 1)
                        ins.then_inc(slots_gated, 1)
                pe.wait_ge(act_ready, i * 2 + 1)
                pe.wait_ge(outputs_ready, i * 2 + 1)
                down_unit(0, n_(8), PRE_U + 8)
                if not last:
                    pe.wait_ge(disp_ready, i + 2)
                    pe.wait_ge(dispT_ready, i + 1)
                    gather(0)
                    pe.wait_ge(gslot_ready, i + 1)
                    gather(1)
                down_unit(1, n_(9), PRE_U + 9)
                if not last:
                    pe.wait_ge(xT_ready, i * 4 + 6)
                turn_gu(i * 2 + 1)
                down_unit(2, n_(10), PRE_U + 10)
                down_unit(3, n_(11), PRE_U + 11)
                if not last:
                    pe.wait_ge(gate_clipped, i * 2 + 2)
                    gather(2)
                    pe.wait_ge(up_clipped, i * 2 + 2)
                    gather(3)
                gap = GU_U if last else 0
                if not last:
                    pe.wait_ge(gu_copied, i * 2 + 2)
                    pe.wait_ge(sel_ready, i * 2 + 3)
                    bias(0)
                    pe.wait_ge(xT_ready, i * 4 + 8)
                    for k in range(GU_U):
                        gu_unit(0, k, n_(12 + k), PRE_U + 12 + k)
                pe.wait_ge(act_ready, i * 2 + 2)
                pe.wait_ge(outputs_ready, i * 2 + 2)
                for u in range(DN_U):
                    down_unit(u, n_(20 + u - gap), PRE_U + 20 + u - gap)
                    if u == 1 and not last:
                        turn_gu(i * 2 + 2)
                    if u == 1 and last:
                        pe.wait_ge(outputs_ready, i * 2 + 2)
                        pe.wait_ge(gu_copied, i * 2 + 2)
                        last_scatter(0)

            def last_scatter(a):
                for job in range(4):
                    ins = mm(ps[:, job, :], dispT[:, a, job // 2, :], ysc[:, a, (job % 2) * 512:(job % 2 + 1) * 512],
                             start=a == 0, stop=a == 1)
                    if a == 1:
                        ins.then_inc(scattered, 1)

            with pe.Fori(0, last_pair) as i:
                iteration(i, False)
            iteration(last_pair, True)
            pe.wait_ge(outputs_ready, last_pair * 2 + 3)
            last_scatter(1)


_INS = ["x", "g_mix", "w_in", "w_pool", "pool_scale", "w_out", "g_ffn", "w_router", "b_router",
        "w_gu", "b_gu", "w_down", "b_down", "g_final"]


def kernel(**inputs):
    import concourse.bacc as bacc
    from concourse.bass_utils import run_bass_kernel_spmd

    nc = bacc.Bacc("TRN2", target_bir_lowering=False, num_devices=1)
    arrays, args = {}, []
    for name in _INS + ["consts"]:
        a = np.ascontiguousarray(constants() if name == "consts" else inputs[name])
        arrays[f"in_{name}"] = a
        args.append(nc.dram_tensor(f"in_{name}", a.shape, mybir.dt.from_np(a.dtype), kind="ExternalInput").ap())
    args.append(nc.dram_tensor("out", (1, T, D), F32, kind="ExternalOutput").ap())
    hybrid_layer(nc, *args)
    r = run_bass_kernel_spmd(nc, [arrays], core_ids=[0])
    return r.results[0]["out"]
```

```python
from contextlib import ExitStack

import concourse.bass as bass
import numpy as np
from concourse import mybir

F32 = mybir.dt.float32
F32R = mybir.dt.float32r
I32 = mybir.dt.int32
U32 = mybir.dt.uint32
ALU = mybir.AluOpType
ACT = mybir.ActivationFunctionType
AX = mybir.AxisListType

P = 128
T, D = 256, 1024
TT = T // P
DC = D // P
DP = 512
DA = 512
H, HD = 8, 64
WINDOWS = (2, 4, 8, 16)
PATTERNS = ((128, 1), (512, 4), (2048, 16))
E, K, FE = 32, 4, 1024
LIMIT, ALPHA, EPS = 7.0, 1.702, 1e-5
NEG = -1e30
SLOTS = 64
PAD = 16
N_IN = DP + 3 * DA

UW = 2048
RAW = 8
SPL = 4
PLACE = (2, 3, 1, 0)
EARLY = 3
GU_U, DN_U = 8, 4
ITER_U = 2 * (GU_U + DN_U)
PRE_U = GU_U
PAIRS = E // 2

_AT, _n = {}, 0
for _name, _w in (("ident", P), ("earlier", P), ("ones", P), ("stack", SLOTS), ("slots", SLOTS), ("experts", E),
                  ("limits", 4), ("selsrc", E), ("count0", P), ("count1", 2 * P), ("invcount", 4 * PAD)):
    _AT[_name] = (_n, _n + _w)
    _n += _w
N_CONST = _n


def constants():
    c = np.zeros((P, N_CONST), np.float32)

    def put(name, a):
        lo, hi = _AT[name]
        c[:a.shape[0], lo:hi] = a

    r = np.arange(P)
    put("ident", np.eye(P))
    put("earlier", r[:, None] < r[None, :])
    put("ones", np.ones((P, P)))
    put("stack", np.concatenate([np.eye(SLOTS)] * 2))
    put("slots", np.tile(np.arange(SLOTS), (P, 1)))
    put("experts", np.tile(np.arange(E), (P, 1)))
    put("limits", np.tile([SLOTS, 2 * SLOTS, 3 * SLOTS, T], (P, 1)))
    put("selsrc", np.concatenate([np.eye(E)] * 4))
    diff = np.arange(T)[:, None] - np.arange(T)[None, :]
    seen = sum(((diff >= 0) & (diff % d == 0) & (diff // d <= w // d)).astype(np.float32) for w, d in PATTERNS)
    put("count0", seen[:P, :P])
    put("count1", seen[P:])
    put("invcount", np.tile(np.concatenate([1.0 / np.minimum(np.arange(PAD) + 1.0, w) for w in WINDOWS]), (P, 1)))
    return c


def hybrid_layer(nc, x, g_mix, w_in, w_pool, pool_scale, w_out, g_ffn, w_router, b_router,
                 w_gu, b_gu, w_down, b_down, g_final, consts, out):
    KB = 1024
    with ExitStack() as ctx:
        def sem(name):
            return ctx.enter_context(nc.semaphore(name))

        base = (nc.sbuf_base + 31) // 32 * 32
        arena_bytes = 207 * KB + 768
        ctx.enter_context(nc.sbuf_tensor("arena", [P, arena_bytes // 4], F32))

        def at(name, shape, dt, off):
            size = 4
            for s in shape[1:]:
                size *= s
            assert off + size <= arena_bytes, (name, off, size)
            return nc.alloc_sbuf_tensor_at(name, shape, dt, offset=base + off)

        raw = at("raw", [P, RAW, UW], F32, 0)
        split = at("split", [P, SPL, 2, UW], F32R, 64 * KB)
        gu = at("gu", [P, 2 * FE], F32, 128 * KB)
        gate = at("gate", [P, DC * SLOTS], F32, 136 * KB)
        sig = at("sig", [P, DC * SLOTS], F32, 138 * KB)
        lin = at("lin", [P, DC * SLOTS], F32, 140 * KB)
        actT = at("actT", [P, DC, 2, SLOTS], F32R, 142 * KB)
        ysc = at("ysc", [P, 2, D], F32, 146 * KB)
        disp = at("disp", [P, TT, 2, 4, SLOTS], F32R, 186 * KB)
        dispT = at("dispT", [P, 2, TT, P], F32, 156 * KB)
        h2h = at("h2h", [P, TT, D], F32R, 158 * KB)
        h2l = at("h2l", [P, TT, D], F32R, 166 * KB)
        acc = at("acc", [P, TT, D], F32, 174 * KB)
        bgu = at("bgu", [P, FE], F32R, 182 * KB)
        xT = at("xT", [P, 2, DC, 2, SLOTS], F32R, 190 * KB)
        outs = at("outs", [P, TT, D], F32, 0)
        junk3 = [at(f"junk3{t}", [P, D], F32, (8 + 4 * t) * KB) for t in range(TT)]
        gfin = at("gfin", [P, D], F32, 16 * KB)
        wout = at("wout", [P, DC, D], F32, 64 * KB)
        wsp = [at(f"wsp{n}", [P, 2, UW], F32R, off * KB) for n, off in enumerate((112, 158))]
        xr = at("xr", [P, TT, D], F32, 96 * KB)
        hTh = at("hTh", [P, DC, T], F32R, 104 * KB)
        hTl = at("hTl", [P, DC, T], F32R, 190 * KB)
        sm1 = at("sm1", [P, H, 2 * P], F32, 96 * KB)
        pr1 = at("pr1", [P, H, 2 * P], F32, 104 * KB)
        h2 = at("h2", [P, TT, D], F32, 64 * KB)
        h2T = at("h2T", [P, DC, T], F32, 72 * KB)
        junk = [at(f"junk{t}", [P, D], F32, (112 + 4 * t) * KB) for t in range(TT)]
        junk2 = [at(f"junk2{t}", [P, D], F32, (128 + 4 * t) * KB) for t in range(TT)]
        qT = at("qT", [P, 4, T], F32, 112 * KB)
        kT = at("kT", [P, 4, T], F32, 116 * KB)
        sm0 = at("sm0", [P, H, P], F32, 120 * KB)
        pr0 = at("pr0", [P, H, P], F32, 124 * KB)
        yat = at("yat", [P, TT, DA], F32, 120 * KB)
        W = PAD + T
        uT = at("uT", [P, 4, W], F32, 128 * KB)
        wsA = at("wsA", [P, 4, W], F32, 128 * KB + 16 * W)
        wsB = at("wsB", [P, 4, W], F32, 128 * KB + 32 * W)
        assert 48 * W <= 13 * KB
        wrt = at("wrt", [P, DC, E], F32, 141 * KB)
        wpool = at("wpool", [P, 4, P], F32, 142 * KB)
        vecs = at("vecs", [2 * DC + 4, P], F32, 144 * KB)
        gffn = at("gffn", [P, D], F32, 150 * KB)
        neg0 = at("neg0", [P, P], F32, 154 * KB)
        neg1 = at("neg1", [P, 2 * P], F32, 154 * KB + 512)
        prT = at("prT", [P, 3 * H, P], F32, 158 * KB)
        braw = at("braw", [P, FE], F32, 186 * KB)
        mixT = at("mixT", [P, DC, T], F32, 190 * KB)
        vau = at("vau", [P, TT, H, HD + 1], F32, 198 * KB)
        onehot = at("onehot", [P, TT, K, E], F32, 128 * KB)
        weighted = at("weighted", [P, TT, K, E], F32, 129 * KB)

        top = [0]

        def small(name, shape, dt=F32):
            size = 4
            for s in shape[1:]:
                size *= s
            top[0] += (size + 31) // 32 * 32
            return at(name, shape, dt, top[0] - (size + 31) // 32 * 32)

        top[0] = 198 * KB + 4 * TT * H * (HD + 1)
        cst = small("cst", [P, N_CONST])
        brt = small("brt", [P, E])
        vecT = small("vecT", [P, 2 * DC + 4])
        identr = small("identr", [P, P], F32R)
        ssq = small("ssq", [P, TT])
        inv = small("inv", [P, TT])
        rs = small("rs", [P, TT])
        mxs = small("mxs", [P, 2, H])
        nmx = small("nmx", [P, 2, H])
        rden = small("rden", [P, 2, H])
        scrap = small("scrap", [P, 1])
        top[0] = 198 * KB
        lg = small("lg", [P, TT, E])
        v8 = small("v8", [P, TT, 8])
        i8 = small("i8", [P, TT, 8], U32)
        i4 = small("i4", [P, TT, K])
        nv1 = small("nv1", [P, TT])
        e4 = small("e4", [P, TT, K])
        s4 = small("s4", [P, TT])
        r4 = small("r4", [P, TT])
        g4 = small("g4", [P, TT, K])
        mask = small("mask", [P, TT, E])
        comb = small("comb", [P, TT, E])
        rank1 = small("rank1", [P, TT, E])
        rank = small("rank", [P, TT, E])
        most = small("most", [P, 1])
        over = small("over", [P, 4])
        nover = small("nover", [P, 1])
        further = small("further", [P, 1], I32)
        cpair = small("cpair", [P, TT, 2])
        gslot = small("gslot", [P, 2])
        sel = small("sel", [P, 2, 2, SLOTS], F32R)
        assert top[0] <= 198 * KB + 4 * TT * H * (HD + 1)

        ps = ctx.enter_context(nc.psum_tensor("ps", [P, 8, 512], F32))
        GU, Y = 0, 4
        M = (6, 7)

        def c_(name, rows=P):
            lo, hi = _AT[name]
            return cst[0:rows, lo:hi]

        def bc(ap, *dims):
            return ap.broadcast_to(list(dims))

        x_loaded = [sem(f"x_loaded{t}") for t in range(TT)]
        raw_loaded = [sem(f"raw_loaded{s}") for s in range(RAW)]
        const_loaded, vec_loaded, wout_loaded = sem("const_loaded"), sem("vec_loaded"), sem("wout_loaded")
        wpool_loaded, router_loaded = sem("wpool_loaded"), sem("router_loaded")
        bgu_loaded, bdown_loaded = sem("bgu_loaded"), sem("bdown_loaded")
        gffn_loaded, gfin_loaded = sem("gffn_loaded"), sem("gfin_loaded")
        out_weighted, out_ready = sem("out_weighted"), [sem(f"out_ready{t}") for t in range(TT)]
        stored = sem("stored")
        squares, inv_ready, rstd_ready, scaled = sem("squares"), sem("inv_ready"), sem("rstd_ready"), sem("scaled")
        dve_step, pool_step = sem("dve_step"), sem("pool_step")
        vec_turned, vec_ready = sem("vec_turned"), sem("vec_ready")
        x_turned, hTh_ready, hTl_ready = sem("x_turned"), sem("hTh_ready"), sem("hTl_ready")
        win_high, win_low, ymix_dve = sem("win_high"), sem("win_low"), sem("ymix_dve")
        u_summed, qk_summed = sem("u_summed"), sem("qk_summed")
        win_used, q_ready, k_ready, u_ready, v_ready = (
            sem("win_used"), sem("q_ready"), sem("k_ready"), sem("u_ready"), sem("v_ready"))
        windows_summed, means_ready = sem("windows_summed"), sem("means_ready")
        pads_ready, pooled_ready, ypool_done, ypool_ready = (
            sem("pads_ready"), sem("pooled_ready"), sem("ypool_done"), sem("ypool_ready"))
        scores, masked, max_ready, exp_done, probs = (
            sem("scores"), sem("masked"), sem("max_ready"), sem("exp_done"), sem("probs"))
        probs_turned, prT_act, prT_dve, attended, yat_ready, yat_turned, ymix_ready = (
            sem("probs_turned"), sem("prT_act"), sem("prT_dve"), sem("attended"), sem("yat_ready"),
            sem("yat_turned"), sem("ymix_ready"))
        half_added = sem("half_added")
        projected, h2_turned, h2T_act, h2T_dve, logits = (
            sem("projected"), sem("h2_turned"), sem("h2T_act"), sem("h2T_dve"), sem("logits"))
        h2h_ready, h2l_ready, bgu_high, bgu_ready, identr_ready = (
            sem("h2h_ready"), sem("h2l_ready"), sem("bgu_high"), sem("bgu_ready"), sem("identr_ready"))
        top_ready, exp4_done, mask_ready, ranked, comb_ready, comb_turned = (
            sem("top_ready"), sem("exp4_done"), sem("mask_ready"), sem("ranked"), sem("comb_ready"),
            sem("comb_turned"))
        rounds_ready, ysc_zeroed, dispT_zeroed = (
            sem("rounds_ready"), sem("ysc_zeroed"), sem("dispT_zeroed"))
        high_ready, low_ready, unit_used = sem("high_ready"), sem("low_ready"), sem("unit_used")
        sel_zeroed, sel_ready, bias_added = sem("sel_zeroed"), sem("sel_ready"), sem("bias_added")
        gu_copied, outputs_ready = sem("gu_copied"), sem("outputs_ready")
        gate_turned, up_turned, gate_clipped, up_clipped = (
            sem("gate_turned"), sem("up_turned"), sem("gate_clipped"), sem("up_clipped"))
        sig_done, gsig_done, act_done, act_high, act_ready = (
            sem("sig_done"), sem("gsig_done"), sem("act_done"), sem("act_high"), sem("act_ready"))
        disp_zeroed = sem("disp_zeroed")
        disp_ready, gathered, xT_ready = sem("disp_ready"), sem("gathered"), sem("xT_ready")
        disp_turned, dispT_ready, slots_gated, gslot_ready = (
            sem("disp_turned"), sem("dispT_ready"), sem("slots_gated"), sem("gslot_ready"))
        scattered, added, pair_taken = sem("scattered"), sem("added"), sem("pair_taken")

        def pair_of(i):
            return i % PAIRS

        block = ctx.enter_context(nc.Block())

        @block.sync
        def _(sp):
            for t in range(TT):
                sp.dma_start(acc[:, t, :], x[0, t * P:(t + 1) * P, :]).then_inc(x_loaded[t], 16)
            sp.dma_start(cst[:], consts).then_inc(const_loaded, 16)
            for c in range(DC):
                sp.dma_start(raw[:, c, :], w_in[0, c * P:(c + 1) * P, :]).then_inc(raw_loaded[c], 16)
            sp.dma_start(wpool[:], w_pool[0].rearrange("g c d -> c g d")).then_inc(wpool_loaded, 16)
            for n in range(4):
                sp.dma_start(braw[n * E:(n + 1) * E, :], b_gu[0, :, n // 2 * FE:(n // 2 + 1) * FE]).then_inc(bgu_loaded, 16)
            sp.dma_start(wout[:], w_out[0].rearrange("(c p) n -> p c n", p=P)).then_inc(wout_loaded, 16)
            sp.dma_start(wrt[:], w_router[0].rearrange("(c p) e -> p c e", p=P)).then_inc(router_loaded, 16)
            sp.dma_start(brt[:], b_router.broadcast_to([P, E])).then_inc(router_loaded, 16)
            sp.dma_start(gffn[:], g_ffn.broadcast_to([P, D])).then_inc(gffn_loaded, 16)
            sp.wait_ge(ysc_zeroed, 1)
            sp.dma_start(ysc[0:E, 0, :], b_down[0]).then_inc(bdown_loaded, 16)

            def load(e, first, slot_unit):
                s = slot_unit % RAW
                if first < GU_U:
                    src = w_gu[0, bass.ds(e, 1), first * P:(first + 1) * P, :].rearrange("a p n -> p (a n)")
                    sp.dma_start(raw[:, s, :], src).then_inc(raw_loaded[s], 16)
                else:
                    u = first - GU_U
                    src = w_down[0, bass.ds(e, 1), 2 * u * P:2 * (u + 1) * P, :].rearrange(
                        "a (r p) n -> p (a r) n", p=P)
                    dst = raw[:, s, :].rearrange("p (r n) -> p r n", r=2)
                    sp.dma_start(dst, src).then_inc(raw_loaded[s], 16)

            for c in range(PRE_U):
                sp.wait_ge(win_low, c + 1)
                load(0, c, c)
            for k in range(EARLY):
                sp.wait_ge(low_ready, k + 1)
                load(1, k, k)
            sp.wait_ge(rounds_ready, 1)
            last_pair = sp.snap(sp.value_load(further[0:1, 0:1], min_val=0, max_val=T // SLOTS - 1) * PAIRS + (PAIRS - 1))

            def iteration(i, last):
                a = pair_of(i) * 2
                nxt = pair_of(i + 1) * 2
                for k in range(EARLY, ITER_U + (0 if last else EARLY)):
                    if last and k in range(GU_U + DN_U, 2 * GU_U + DN_U):
                        continue
                    at_ = k - (GU_U if last and k >= 2 * GU_U + DN_U else 0)
                    sp.wait_ge(low_ready, i * ITER_U + at_ + 1)
                    if k < GU_U:
                        load(a + 1, k, at_)
                    elif k < GU_U + DN_U:
                        load(a, k, at_)
                    elif k < 2 * GU_U + DN_U:
                        load(nxt, k - GU_U - DN_U, at_)
                    elif k < ITER_U:
                        load(a + 1, k - GU_U - DN_U, at_)
                    else:
                        load(nxt + 1, k - ITER_U, at_)

            with sp.Fori(0, last_pair) as i:
                iteration(i, False)
            iteration(last_pair, True)
            sp.wait_ge(low_ready, last_pair * ITER_U + PRE_U + 12)
            sp.dma_start(gfin[:], g_final.rearrange("(a n) -> a n", a=1).broadcast_to([P, D])).then_inc(gfin_loaded, 16)
            for t in (1, 0):
                sp.wait_ge(out_ready[t], 1)
                sp.dma_start(out[0, t * P:(t + 1) * P, :], outs[:, t, :]).then_inc(stored, 16)
            sp.wait_ge(stored, 16 * TT)

        @block.gpsimd
        def _(pool):
            steps = [0]

            def link(ins):
                steps[0] += 1
                ins.then_inc(pool_step, 1)
                pool.wait_ge(pool_step, steps[0])

            pool.memset(uT[:, :, 0:PAD], 0.0).then_inc(pads_ready, 1)
            pool.memset(vau[:, :, :, HD:HD + 1], 1.0).then_inc(pads_ready, 1)
            pool.memset(ysc[:, 0, :], 0.0).then_inc(ysc_zeroed, 1)
            pool.wait_ge(const_loaded, 16)
            pool.wait_ge(u_ready, 1)
            pool.wait_ge(pads_ready, 2)
            link(pool.tensor_tensor(wsA[:, :, 1:W], uT[:, :, 1:W], uT[:, :, 0:W - 1], ALU.add))
            link(pool.tensor_tensor(wsB[:, 1:4, 3:W], wsA[:, 1:4, 3:W], wsA[:, 1:4, 1:W - 2], ALU.add))
            link(pool.tensor_tensor(wsA[:, 2:4, 7:W], wsB[:, 2:4, 7:W], wsB[:, 2:4, 3:W - 4], ALU.add))
            pool.tensor_tensor(wsB[:, 3:4, 15:W], wsA[:, 3:4, 15:W], wsA[:, 3:4, 7:W - 8], ALU.add).then_inc(windows_summed, 1)
            pool.wait_ge(windows_summed, 1)
            pool.wait_ge(win_used, DC)
            for g, w in enumerate(WINDOWS):
                ins = pool.tensor_tensor(mixT[:, 4 + g, 0:PAD], (wsA, wsB)[g % 2][:, g, PAD:2 * PAD],
                                         c_("invcount")[:, g * PAD:(g + 1) * PAD], ALU.mult)
            link(ins)
            pool.wait_ge(means_ready, 1)
            pool.tensor_tensor(mixT[:, 4:8, :], mixT[:, 4:8, :], uT[:, :, PAD:W], ALU.subtract).then_inc(pooled_ready, 1)
            def tokens_low(t):
                pool.wait_ge(h2h_ready, t + 1)
                pool.tensor_tensor(h2l[:, t, :], h2[:, t, :], h2h[:, t, :].bitcast(F32), ALU.subtract).then_inc(h2l_ready, 1)

            pool.wait_ge(bgu_ready, 1)
            pool.memset(disp[:, :, :, 0, :].bitcast(F32), 0.0).then_inc(disp_zeroed, 1)
            pool.memset(disp[:, :, :, 3, :].bitcast(F32), 0.0).then_inc(disp_zeroed, 1)
            tokens_low(0)
            pool.wait_ge(projected, 3)
            pool.memset(sel[:].bitcast(F32), 0.0).then_inc(sel_zeroed, 1)
            pool.memset(dispT[:], 0.0).then_inc(dispT_zeroed, 1)
            pool.wait_ge(scaled, 2 * TT)
            pool.memset(ysc[:, 1, :], 0.0).then_inc(ysc_zeroed, 1)
            def select(e, half):
                src = c_("selsrc")[:, bass.ds(e, 1)]
                pool.wait_ge(sel_zeroed, 1)
                pool.tensor_tensor(sel[:, half, 0, :], bc(src, P, SLOTS), c_("ones")[:, 0:SLOTS],
                                   ALU.mult).then_inc(sel_ready, 1)

            select(0, 0)
            tokens_low(1)
            pool.wait_ge(rounds_ready, 1)
            last_pair = pool.snap(pool.value_load(further[0:1, 0:1], min_val=0, max_val=T // SLOTS - 1) * PAIRS + (PAIRS - 1))

            with pool.Fori(0, last_pair) as i:
                pool.wait_ge(bias_added, i * 2 + 1)
                select(pair_of(i) * 2 + 1, 1)
                pool.wait_ge(bias_added, i * 2 + 1)
                select(pair_of(i + 1) * 2, 0)
            i = last_pair
            pool.wait_ge(bias_added, i * 2 + 1)
            select(pair_of(i) * 2 + 1, 1)
            pool.wait_ge(gfin_loaded, 16)
            pool.wait_ge(added, last_pair * 4 + 6 + TT)
            pool.tensor_tensor(outs[:, 0, :], acc[:, 0, :], gfin[:], ALU.mult).then_inc(out_weighted, 1)

        @block.scalar
        def _(act):
            act.dma_start(vecs[0:DC, :], g_mix.rearrange("a (c p) -> (a c) p", p=P)).then_inc(vec_loaded, 16)
            act.dma_start(vecs[DC:DC + 4, :], pool_scale.rearrange("a (c p) -> (a c) p", p=P)).then_inc(vec_loaded, 16)
            act.dma_start(vecs[DC + 4:2 * DC + 4, :], g_ffn.rearrange("a (c p) -> (a c) p", p=P)).then_inc(vec_loaded, 16)

            def high(n, k, first_use):
                act.wait_ge(raw_loaded[k % RAW], (first_use + 1) * 16)
                if not isinstance(n, int) or n >= SPL:
                    act.wait_ge(unit_used, n - SPL + 1)
                act.activation(split[:, PLACE[k % SPL], 0, :], raw[:, k % RAW, :], ACT.Copy).then_inc(high_ready, 1)


            act.wait_ge(const_loaded, 16)
            act.activation(scrap[:], c_("ones")[:, 0:1], ACT.Sqrt)
            for t in range(TT):
                act.wait_ge(x_loaded[t], 16)
            for t in range(TT):
                act.activation(junk[t][:], acc[:, t, :], ACT.Square, accum_out=ssq[:, t:t + 1]).then_inc(squares, 1)
            act.wait_ge(inv_ready, 1)
            act.activation(rs[:], inv[:], ACT.Sqrt).then_inc(rstd_ready, 1)

            def win_part(c):
                act.wait_ge(raw_loaded[c], 16)
                if c >= 2:
                    act.wait_ge(win_used, c - 1)
                act.activation(wsp[c % 2][:, 0, :], raw[:, c, :], ACT.Copy).then_inc(win_high, 1)

            win_part(0)
            act.wait_ge(vec_ready, 1)
            for b in range(4):
                act.wait_ge(x_turned, b + 1)
                for c in (2 * b, 2 * b + 1):
                    ins = act.activation(hTh[:, c, :], ps[:, b, (c % 2) * T:(c % 2 + 1) * T], ACT.Copy,
                                         scale=vecT[:, c:c + 1])
                ins.then_inc(hTh_ready, 1)
            for c in range(1, DC):
                win_part(c)
                if c == 5:
                    act.wait_ge(bgu_loaded, 64)
                    act.activation(bgu[:], braw[:], ACT.Copy).then_inc(bgu_high, 1)
                    act.wait_ge(const_loaded, 16)
                    act.activation(identr[:], c_("ident"), ACT.Copy).then_inc(identr_ready, 1)
            act.wait_ge(u_summed, 1)
            act.activation(uT[:, :, PAD:W], ps[:, 4:6, :].rearrange("p a (b t) -> p (a b) t", b=2),
                           ACT.Copy).then_inc(u_ready, 1)
            act.wait_ge(qk_summed, 1)
            act.activation(qT[:].rearrange("p c t -> p (c t)"), ps[:, 0:2, :].rearrange("p a b -> p (a b)"),
                           ACT.Copy).then_inc(q_ready, 1)

            def exps(tile, pr, sm):
                act.wait_ge(max_ready, tile + 1)
                for s in range(H):
                    ins = act.activation(pr[:, s, :], sm[:, s, :], ACT.Exp, bias=nmx[:, tile, s:s + 1])
                ins.then_inc(exp_done, 1)

            act.wait_ge(windows_summed, 1)
            act.wait_ge(win_used, DC)
            for g, w in enumerate(WINDOWS):
                ins = act.activation(mixT[:, 4 + g, PAD:T], (wsA, wsB)[g % 2][:, g, 2 * PAD:W], ACT.Copy, scale=1.0 / w)
            ins.then_inc(means_ready, 1)
            exps(0, pr1, sm1)
            act.wait_ge(ypool_done, 1)
            for g in range(4):
                ins = act.activation(mixT[:, g, :], ps[:, 6 + g // 2, (g % 2) * T:(g % 2 + 1) * T], ACT.Copy,
                                     scale=vecT[:, DC + g:DC + g + 1])
            ins.then_inc(ypool_ready, 1)
            exps(1, pr0, sm0)
            for n in (0, 2, 4):
                act.wait_ge(probs_turned, n + 1)
                act.activation(prT[:, 4 * n:4 * n + 4, :].rearrange("p a b -> p (a b)"), ps[:, 4 + n % 4, :],
                               ACT.Copy).then_inc(prT_act, 1)
            act.wait_ge(yat_turned, 1)
            act.activation(mixT[:, 4:6, :].rearrange("p a b -> p (a b)"), ps[:, 6, :], ACT.Copy).then_inc(ymix_ready, 1)
            high(0, 0, 1)
            high(1, 1, 1)
            def sum_squares(t):
                act.wait_ge(added, 1 + t)
                act.activation(junk2[t][:], acc[:, t, :], ACT.Square, accum_out=ssq[:, t:t + 1]).then_inc(squares, 1)

            def turned_scaled(t):
                act.wait_ge(h2_turned, 2 * t + 1)
                for c in range(4):
                    ins = act.activation(h2T[:, c, t * P:(t + 1) * P], ps[:, 4 + 2 * t, c * P:(c + 1) * P], ACT.Copy,
                                         scale=vecT[:, DC + 4 + c:DC + 5 + c])
                ins.then_inc(h2T_act, 1)

            def root(t):
                act.wait_ge(inv_ready, t + 2)
                act.activation(rs[:, t:t + 1], inv[:, t:t + 1], ACT.Sqrt).then_inc(rstd_ready, 1)

            def tokens_high(t):
                act.wait_ge(scaled, TT + t + 1)
                act.activation(h2h[:, t, :], h2[:, t, :], ACT.Copy).then_inc(h2h_ready, 1)

            sum_squares(0)
            turned_scaled(0)
            root(0)
            tokens_high(0)
            turned_scaled(1)
            sum_squares(1)
            root(1)
            act.activation(scrap[:], c_("ones")[:, 0:1], ACT.Exp)
            tokens_high(1)
            act.wait_ge(top_ready, 1)
            for t in range(TT):
                act.activation(e4[:, t, :], v8[:, t, 0:K], ACT.Exp, bias=nv1[:, t:t + 1],
                               accum_out=s4[:, t:t + 1]).then_inc(exp4_done, 1)
            high(2, 2, 1)

            def gather_copy(job, count):
                act.wait_ge(gathered, count)
                act.activation(xT[:, :, 2 * job:2 * job + 2].rearrange("p e c a s -> p e (c a s)"),
                               ps[:, M[job % 2], :].rearrange("p (e n) -> p e n", e=2), ACT.Copy).then_inc(xT_ready, 1)

            def gu_copy(e, used):
                act.wait_ge(unit_used, used)
                if not isinstance(e, int):
                    act.wait_ge(up_turned, e)
                act.activation(gu[:], ps[:, 0:4, :].rearrange("p a b -> p (a b)"), ACT.Copy).then_inc(gu_copied, 1)

            def sigmoid(e):
                act.wait_ge(gate_clipped, e + 1)
                act.activation(sig[:], gate[:], ACT.Sigmoid, scale=ALPHA).then_inc(sig_done, 1)

            def act_split(e, used=None):
                act.wait_ge(act_done, e + 1)
                if used is not None:
                    act.wait_ge(unit_used, used)
                act.activation(actT[:, :, 0, :], lin[:].rearrange("p (c s) -> p c s", s=SLOTS),
                               ACT.Copy).then_inc(act_high, 1)

            def y_copy(i, half, used):
                act.wait_ge(unit_used, used)
                act.wait_ge(gslot_ready, i + 1)
                act.wait_ge(scattered, i * 4 + 4)
                act.activation(ysc[:, half, :], ps[:, Y:Y + 2, :].rearrange("p a b -> p (a b)"), ACT.Copy,
                               scale=gslot[:, half:half + 1]).then_inc(outputs_ready, 1)

            act.wait_ge(h2l_ready, 2)
            high(3, 3, 1)
            gather_copy(0, 1)
            gather_copy(1, 2)
            high(4, 4, 1)
            high(5, 5, 1)
            gather_copy(2, 3)
            high(6, 6, 1)
            gather_copy(3, 4)
            high(7, 7, 1)

            def unit(i, k, skipped=0):
                k -= skipped
                high(i * ITER_U + PRE_U + k, PRE_U + k, i * (ITER_U // RAW) + 2 + k // RAW)

            unit(0, 0)
            unit(0, 1)
            gu_copy(0, PRE_U)
            act.wait_ge(rounds_ready, 1)
            last_pair = act.snap(act.value_load(further[0:1, 0:1], min_val=0, max_val=T // SLOTS - 1) * PAIRS + (PAIRS - 1))

            sigmoid(0)

            def used(i, k):
                return i * ITER_U + (PRE_U + k)

            def iteration(i, last):
                unit(i, 2)
                unit(i, 3)
                unit(i, 4)
                act_split(i * 2)
                for k in range(5, 10):
                    unit(i, k)
                gu_copy(i * 2 + 1, used(i, GU_U))
                unit(i, 10)
                if not last:
                    gather_copy(0, i * 4 + 5)
                    gather_copy(1, i * 4 + 6)
                unit(i, 11)
                if last:
                    unit(i, 20, GU_U)
                    unit(i, 21, GU_U)
                    sigmoid(i * 2 + 1)
                    y_copy(i, 0, used(i, 12))
                    act_split(i * 2 + 1, used(i, 12))
                    unit(i, 22, GU_U)
                    unit(i, 23, GU_U)
                    act.activation(scrap[:], c_("ones")[:, 0:1], ACT.Sqrt)
                else:
                    unit(i, 12)
                    unit(i, 13)
                    sigmoid(i * 2 + 1)
                    y_copy(i, 0, used(i, 12))
                    gather_copy(2, i * 4 + 7)
                    gather_copy(3, i * 4 + 8)
                    for k in range(14, 18):
                        unit(i, k)
                    act_split(i * 2 + 1, used(i, 12))
                    for k in range(18, 22):
                        unit(i, k)
                    gu_copy(i * 2 + 2, used(i, 20))
                    unit(i, 22)
                    unit(i, 23)
                    unit(i, 24)
                    unit(i, 25)
                    sigmoid(i * 2 + 2)
                if not last:
                    y_copy(i, 1, used(i, 24))
                else:
                    act.wait_ge(unit_used, used(i, 24 - GU_U))
                    act.wait_ge(gslot_ready, i + 1)
                    act.activation(ysc[:, 1, 0:512], ps[:, Y, :], ACT.Copy, scale=gslot[:, 1:2]).then_inc(outputs_ready, 1)

            with act.Fori(0, last_pair) as i:
                iteration(i, False)
            iteration(last_pair, True)
            for t in range(TT):
                act.wait_ge(added, last_pair * 4 + 6 + TT + 2 * t)
                act.activation(junk3[t][:], acc[:, t, :], ACT.Square, accum_out=ssq[:, t:t + 1]).then_inc(squares, 1)
            for t in range(TT):
                act.wait_ge(inv_ready, 4 + t)
                act.activation(rs[:, t:t + 1], inv[:, t:t + 1], ACT.Sqrt).then_inc(rstd_ready, 1)
            act.wait_ge(rstd_ready, 4)
            act.wait_ge(out_weighted, 1)
            act.activation(outs[:, 0, :], outs[:, 0, :], ACT.Copy, scale=rs[:, 0:1]).then_inc(out_ready[0], 1)

        @block.vector
        def _(dve):
            steps = [0]

            def link(ins):
                steps[0] += 1
                ins.then_inc(dve_step, 1)
                dve.wait_ge(dve_step, steps[0])


            def low(n, k):
                dve.wait_ge(high_ready, n + 1)
                dve.tensor_tensor(split[:, PLACE[k % SPL], 1, :], raw[:, k % RAW, :], split[:, PLACE[k % SPL], 0, :].bitcast(F32),
                                  ALU.subtract).then_inc(low_ready, 1)

            dve.wait_ge(const_loaded, 16)
            dve.tensor_scalar(neg0[:], c_("count0"), 0.0, NEG, ALU.is_equal, ALU.mult)
            link(dve.tensor_scalar(neg1[:], c_("count1"), 0.0, NEG, ALU.is_equal, ALU.mult))
            dve.wait_ge(squares, 2)
            link(dve.tensor_scalar(inv[:], ssq[:], 1.0 / D, EPS, ALU.mult, ALU.add))
            dve.reciprocal(inv[:], inv[:]).then_inc(inv_ready, 1)
            dve.wait_ge(rstd_ready, 1)
            for t in range(TT):
                dve.tensor_scalar(xr[:, t, :], acc[:, t, :], rs[:, t:t + 1], None, ALU.mult).then_inc(scaled, 1)
            dve.wait_ge(vec_turned, 1)
            dve.tensor_copy(vecT[:], ps[:, 7, 0:2 * DC + 4]).then_inc(vec_ready, 1)
            dve.wait_ge(vec_ready, 1)

            def win_rest(c):
                dve.wait_ge(win_high, c + 1)
                dve.tensor_tensor(wsp[c % 2][:, 1, :], raw[:, c, :], wsp[c % 2][:, 0, :].bitcast(F32),
                                  ALU.subtract).then_inc(win_low, 1)

            win_rest(0)
            for b in range(4):
                dve.wait_ge(hTh_ready, b + 1)
                for c in (2 * b, 2 * b + 1):
                    ins = dve.scalar_tensor_tensor(
                        out=hTl[:, c, :], in0=ps[:, b, (c % 2) * T:(c % 2 + 1) * T], scalar=vecT[:, c:c + 1],
                        in1=hTh[:, c, :].bitcast(F32), op0=ALU.mult, op1=ALU.subtract)
                ins.then_inc(hTl_ready, 1)
            for c in range(1, DC):
                win_rest(c)
                if c == 6:
                    dve.wait_ge(bgu_high, 1)
                    for r in (E, 3 * E):
                        ins = dve.tensor_tensor(bgu[r:r + E, :], braw[r:r + E, :], bgu[r:r + E, :].bitcast(F32),
                                                ALU.subtract)
                    ins.then_inc(bgu_ready, 1)
            dve.wait_ge(qk_summed, 1)
            dve.tensor_copy(kT[:].rearrange("p c t -> p (c t)"),
                            ps[:, 2:4, :].rearrange("p a b -> p (a b)")).then_inc(k_ready, 1)
            dve.wait_ge(win_used, DC)
            for t in range(TT):
                ins = dve.tensor_copy(vau[:, t, :, 0:HD], ps[:, 6 + t, :].rearrange("p (h d) -> p h d", h=H))
            ins.then_inc(v_ready, 1)

            def mask_and_max(n, sm, bank, neg, keys):
                dve.wait_ge(scores, n + 1)
                dve.scalar_tensor_tensor(
                    out=sm[:], in0=ps[:, bank:bank + H * keys // 512, :].rearrange("p a (b k) -> p (a b) k", k=keys),
                    scalar=HD ** -0.5, in1=bc(neg[:].rearrange("p (a k) -> p a k", a=1), P, H, keys),
                    op0=ALU.mult, op1=ALU.add).then_inc(masked, 1)
                dve.wait_ge(masked, n + 1)
                link(dve.tensor_reduce(mxs[:, n, :], sm[:], AX.X, ALU.max))
                dve.tensor_scalar(nmx[:, n, :], mxs[:, n, :], -1.0, None, ALU.mult).then_inc(max_ready, 1)

            def times_count(n, pr, count, keys):
                dve.wait_ge(exp_done, n + 1)
                dve.tensor_tensor(pr[:], pr[:], bc(c_(count).rearrange("p (a k) -> p a k", a=1), P, H, keys),
                                  ALU.mult).then_inc(probs, 1)

            mask_and_max(0, sm1, 0, neg1, 2 * P)
            mask_and_max(1, sm0, 4, neg0, P)
            times_count(0, pr1, "count1", 2 * P)
            times_count(1, pr0, "count0", P)
            for n in (1, 3, 5):
                dve.wait_ge(probs_turned, n + 1)
                dve.tensor_copy(prT[:, 4 * n:4 * n + 4, :].rearrange("p a b -> p (a b)"),
                                ps[:, 4 + n % 4, :]).then_inc(prT_dve, 1)
            for n in range(2):
                dve.wait_ge(attended, n + 1)
                o = ps[:, 6 - 2 * n:8 - 2 * n, 0:4 * (HD + 1)].rearrange("p a (h d) -> p a h d", d=HD + 1)
                link(dve.reciprocal(rden[:, n, :].rearrange("p (a h) -> p a h", a=2), o[:, :, :, HD]))
                for half in range(2):
                    r = rden[:, n, 4 * half:4 * half + 4].rearrange("p (h a) -> p h a", a=1)
                    ins = dve.tensor_tensor(
                        yat[:, 1 - n, half * 256:half * 256 + 256].rearrange("p (h d) -> p h d", d=HD),
                        o[:, half, :, 0:HD], bc(r, P, 4, HD), ALU.mult)
                ins.then_inc(yat_ready, 1)
            dve.wait_ge(yat_turned, 1)
            dve.tensor_copy(mixT[:, 6:8, :].rearrange("p a b -> p (a b)"), ps[:, 7, :]).then_inc(ymix_dve, 1)
            low(0, 0)
            low(1, 1)
            def add_mixer(t, lo, hi, count):
                dve.wait_ge(projected, count)
                return dve.tensor_tensor(acc[:, t, lo * 512:hi * 512],
                                         ps[:, 2 * t + lo:2 * t + hi, :].rearrange("p a b -> p (a b)"),
                                         acc[:, t, lo * 512:hi * 512], ALU.add)

            def turned_scaled(t):
                dve.wait_ge(h2_turned, 2 * t + 2)
                for c in range(4, DC):
                    ins = dve.tensor_scalar(h2T[:, c, t * P:(t + 1) * P], ps[:, 5 + 2 * t, (c - 4) * P:(c - 3) * P],
                                            vecT[:, DC + 4 + c:DC + 5 + c], None, ALU.mult)
                ins.then_inc(h2T_dve, 1)

            def inverse_tile(t, count):
                dve.wait_ge(squares, count + 1)
                link(dve.tensor_scalar(inv[:, t:t + 1], ssq[:, t:t + 1], 1.0 / D, EPS, ALU.mult, ALU.add))
                dve.reciprocal(inv[:, t:t + 1], inv[:, t:t + 1]).then_inc(inv_ready, 1)

            def normalise(t):
                dve.wait_ge(rstd_ready, t + 2)
                dve.scalar_tensor_tensor(out=h2[:, t, :], in0=acc[:, t, :], scalar=rs[:, t:t + 1], in1=gffn[:],
                                         op0=ALU.mult, op1=ALU.mult).then_inc(scaled, 1)

            def top(t):
                dve.wait_ge(logits, t + 1)
                link(dve.scalar_tensor_tensor(out=lg[:, t, :], in0=ps[:, t, 0:E], scalar=rs[:, t:t + 1],
                                              in1=brt[:], op0=ALU.mult, op1=ALU.add))
                link(dve.max(v8[:, t, :], lg[:, t, :]))
                link(dve.max_index(i8[:, t, :], v8[:, t, :], lg[:, t, :]))

            add_mixer(0, 0, 2, 1).then_inc(added, 1)
            add_mixer(1, 0, 1, 2).then_inc(half_added, 1)
            dve.wait_ge(gffn_loaded, 16)
            dve.wait_ge(router_loaded, 32)
            turned_scaled(0)
            inverse_tile(0, 2)
            normalise(0)
            add_mixer(1, 1, 2, 3).then_inc(added, 1)
            turned_scaled(1)
            top(0)
            inverse_tile(1, 3)
            normalise(1)
            top(1)
            dve.tensor_scalar(nv1[:], v8[:, :, 0], -1.0, None, ALU.mult).then_inc(top_ready, 1)
            link(dve.tensor_copy(i4[:], i8[:, :, 0:K]))
            link(dve.tensor_tensor(onehot[:].rearrange("p t k e -> p (t k) e"),
                                   bc(c_("experts").rearrange("p (a e) -> p a e", a=1), P, TT * K, E),
                                   bc(i4[:].rearrange("p t (k a) -> p (t k) a", a=1), P, TT * K, E), ALU.is_equal))
            dve.tensor_reduce(mask[:], onehot[:].rearrange("p t k e -> p t e k"), AX.X, ALU.add).then_inc(mask_ready, 1)
            dve.wait_ge(exp4_done, 2)
            link(dve.reciprocal(r4[:], s4[:]))
            link(dve.tensor_tensor(g4[:], e4[:], bc(r4[:].rearrange("p (t a) -> p t a", a=1), P, TT, K), ALU.mult))
            link(dve.tensor_tensor(weighted[:].rearrange("p t k e -> p (t k) e"),
                                   onehot[:].rearrange("p t k e -> p (t k) e"),
                                   bc(g4[:].rearrange("p t (k a) -> p (t k) a", a=1), P, TT * K, E), ALU.mult))
            dve.tensor_reduce(comb[:], weighted[:].rearrange("p t k e -> p t e k"), AX.X, ALU.add).then_inc(comb_ready, 1)
            dve.wait_ge(ranked, 1)
            dve.wait_ge(mask_ready, 1)
            link(dve.scalar_tensor_tensor(out=rank1[:], in0=ps[:, 5, 0:TT * E].rearrange("p (t e) -> p t e", t=TT),
                                          scalar=1.0, in1=mask[:], op0=ALU.add, op1=ALU.mult))
            link(dve.tensor_scalar(rank[:], rank1[:], -1.0, None, ALU.add))
            def build_disp(e):
                for t in range(TT):
                    mine = rank[:, t, bass.ds(e, 2)].rearrange("p (a b) -> p a b", b=1)
                    for copy in range(2):
                        ins = dve.tensor_tensor(disp[:, t, :, 1 + copy, :],
                                                bc(c_("slots").rearrange("p (a s) -> p a s", a=1), P, 2, SLOTS),
                                                bc(mine, P, 2, SLOTS), ALU.is_equal)
                ins.then_inc(disp_ready, 1)

            def next_round(e, count):
                dve.tensor_copy(cpair[:], comb[:, :, bass.ds(e, 2)])
                dve.wait_ge(disp_ready, count)
                dve.tensor_scalar(rank[:, :, bass.ds(e, 2)], rank[:, :, bass.ds(e, 2)], -float(SLOTS), None,
                                  ALU.add).then_inc(pair_taken, 1)

            dve.wait_ge(comb_ready, 1)
            dve.wait_ge(disp_zeroed, 2)
            build_disp(0)
            next_round(0, 1)
            link(dve.tensor_reduce(most[:], ps[:, 5, TT * E:TT * E + E], AX.X, ALU.max))
            link(dve.tensor_scalar(over[:], c_("limits"), most[:, 0:1], None, ALU.is_lt))
            link(dve.tensor_reduce(nover[:], over[:], AX.X, ALU.add))
            dve.tensor_copy(further[:], nover[:]).then_inc(rounds_ready, 1)
            low(2, 2)
            dve.wait_ge(rounds_ready, 1)
            last_pair = dve.snap(dve.value_load(further[0:1, 0:1], min_val=0, max_val=T // SLOTS - 1) * PAIRS + (PAIRS - 1))
            dve.wait_ge(comb_turned, 1)
            dve.wait_ge(dispT_zeroed, 1)
            dve.tensor_copy(dispT[0:E, 0, :, :], ps[0:E, 4, 0:T].rearrange("p (t q) -> p t q", t=TT)).then_inc(outputs_ready, 1)

            def clip(e):
                dve.wait_ge(gate_turned, e + 1)
                dve.tensor_scalar(gate[:], ps[:, M[0], :], LIMIT, None, ALU.min).then_inc(gate_clipped, 1)
                dve.wait_ge(up_turned, e + 1)
                dve.tensor_scalar(lin[:], ps[:, M[1], :], -LIMIT, LIMIT, ALU.max, ALU.min).then_inc(up_clipped, 1)

            def swiglu(e):
                dve.wait_ge(sig_done, e + 1)
                dve.tensor_tensor(sig[:], gate[:], sig[:], ALU.mult).then_inc(gsig_done, 1)
                dve.wait_ge(gsig_done, e + 1)
                dve.scalar_tensor_tensor(out=lin[:], in0=lin[:], scalar=1.0, in1=sig[:], op0=ALU.add,
                                         op1=ALU.mult).then_inc(act_done, 1)

            def act_low(e):
                dve.wait_ge(act_high, e + 1)
                dve.tensor_tensor(actT[:, :, 1, :], lin[:].rearrange("p (c s) -> p c s", s=SLOTS),
                                  actT[:, :, 0, :].bitcast(F32), ALU.subtract).then_inc(act_ready, 1)

            def add_scattered(i, job):
                dve.wait_ge(scattered, i * 4 + job + 1)
                part = acc[:, job // 2, (job % 2) * 512:(job % 2 + 1) * 512]
                dve.tensor_tensor(part, ps[:, M[job % 2], :], part, ALU.add).then_inc(added, 1)

            for k in range(3, PRE_U + 2):
                low(k, k)
            clip(0)

            def iteration(i, last):
                def unit(k, skipped=0):
                    low(i * ITER_U + (PRE_U + k - skipped), PRE_U + k - skipped)

                swiglu(i * 2)
                unit(2)
                unit(3)
                act_low(i * 2)
                add_scattered(i, 0)
                add_scattered(i, 1)
                unit(4)
                add_scattered(i, 2)
                add_scattered(i, 3)
                unit(5)
                unit(6)
                dve.wait_ge(disp_turned, i + 1)
                dve.tensor_copy(dispT[:].rearrange("p a t q -> p (a t q)"), ps[:, M[0], :]).then_inc(dispT_ready, 1)
                unit(7)
                dve.wait_ge(slots_gated, i + 1)
                dve.tensor_copy(gslot[:], ps[:, M[1], 0:2]).then_inc(gslot_ready, 1)
                if not last:
                    dve.wait_ge(pair_taken, i + 1)
                    e = dve.snap(pair_of(i + 1) * 2)
                    build_disp(e)
                    next_round(e, i + 2)
                unit(8)
                unit(9)
                unit(10)
                unit(11)
                clip(i * 2 + 1)
                if last:
                    unit(20, GU_U)
                    swiglu(i * 2 + 1)
                    unit(21, GU_U)
                    act_low(i * 2 + 1)
                    unit(22, GU_U)
                    unit(23, GU_U)
                else:
                    unit(12)
                    unit(13)
                    unit(14)
                    swiglu(i * 2 + 1)
                    unit(15)
                    unit(16)
                    act_low(i * 2 + 1)
                    for k in range(17, 24):
                        unit(k)
                    clip(i * 2 + 2)
                    unit(24)
                    unit(25)

            with dve.Fori(0, last_pair) as i:
                iteration(i, False)
            iteration(last_pair, True)
            dve.wait_ge(unit_used, (last_pair + 1) * ITER_U)
            dve.wait_ge(gslot_ready, last_pair + 1)
            dve.tensor_scalar(ysc[:, 1, 512:D], ps[:, Y + 1, :], gslot[:, 1:2], None, ALU.mult).then_inc(outputs_ready, 1)
            for job in range(4):
                dve.wait_ge(scattered, last_pair * 4 + job + 5)
                part = acc[:, job // 2, (job % 2) * 512:(job % 2 + 1) * 512]
                dve.tensor_tensor(part, ps[:, job, :], part, ALU.add).then_inc(added, 1)
            dve.wait_ge(gfin_loaded, 16)
            inverse_tile(0, 2 * TT)
            dve.wait_ge(added, last_pair * 4 + 8 + TT)
            link(dve.tensor_tensor(outs[:, 1, :], acc[:, 1, :], gfin[:], ALU.mult))
            inverse_tile(1, 2 * TT + 1)
            dve.wait_ge(rstd_ready, 5)
            dve.tensor_scalar(outs[:, 1, :], outs[:, 1, :], rs[:, 1:2], None, ALU.mult).then_inc(out_ready[1], 1)

        @block.tensor
        def _(pe):
            def mm(out_, lhsT, rhs, start=True, stop=True, shared=False):
                return pe.matmul(out_, lhsT, rhs, start=start, stop=stop, skip_group_check=shared)

            def stay_awake(n, bank=3):
                for _ in range(n):
                    mm(ps[:, bank, :], c_("ident"), cst[:, 0:512])

            pe.wait_ge(const_loaded, 16)
            stay_awake(2)
            pe.wait_ge(vec_loaded, 48)
            pe.transpose(ps[:, 7, 0:2 * DC + 4], vecs[:], c_("ident", 2 * DC + 4)[:, 0:2 * DC + 4]).then_inc(vec_turned, 1)

            def turn(src, done):
                for c in range(DC):
                    for t in range(TT):
                        ins = pe.transpose(ps[:, c // 2, (c % 2) * T + t * P:(c % 2) * T + (t + 1) * P],
                                           src[:, t, c * P:(c + 1) * P], c_("ident"))
                    if c % 2:
                        ins.then_inc(done, 1)

            pe.wait_ge(scaled, 2)
            turn(xr, x_turned)
            def by_channel(c, bank, column):
                wh, wl = wsp[c % 2][:, 0, :], wsp[c % 2][:, 1, :]
                first, last = c == 0, c == DC - 1
                for j in range(4):
                    o = ps[:, bank + j // 2, (j % 2) * T:(j % 2 + 1) * T]
                    cols = slice(column + j * P, column + (j + 1) * P)
                    mm(o, wh[:, cols], hTh[:, c, :], start=first and j % 2 == 0, stop=False, shared=True)
                    mm(o, wh[:, cols], hTl[:, c, :], start=False, stop=False, shared=True)
                    ins = mm(o, wl[:, cols], hTh[:, c, :], start=False, stop=last, shared=True)
                return ins

            def by_token(c):
                wh, wl = wsp[c % 2][:, 0, :], wsp[c % 2][:, 1, :]
                first, last = c == 0, c == DC - 1
                for t in range(TT):
                    o, cols, tok = ps[:, 6 + t, :], slice(DP + 2 * DA, N_IN), slice(t * P, (t + 1) * P)
                    mm(o, hTh[:, c, tok], wh[:, cols], start=first, stop=False)
                    mm(o, hTh[:, c, tok], wl[:, cols], start=False, stop=False)
                    ins = mm(o, hTl[:, c, tok], wh[:, cols], start=False, stop=last)
                return ins

            for c in range(DC):
                if c < 2:
                    pe.wait_ge(hTl_ready, 1)
                pe.wait_ge(win_low, c + 1)
                u = by_channel(c, 4, 0)
                if c == 0:
                    pe.wait_ge(vec_ready, 1)
                    by_token(c)
                    pe.wait_ge(hTl_ready, 4)
                by_channel(c, 0, DP)
                qk = by_channel(c, 2, DP + DA)
                if c == DC - 1:
                    u.then_inc(u_summed, 1)
                    qk.then_inc(qk_summed, 1)
                (by_token(c) if c else qk).then_inc(win_used, 1)
            pe.wait_ge(q_ready, 1)
            pe.wait_ge(k_ready, 1)
            for n, (bank, keys) in enumerate(((0, 2 * P), (4, P))):
                if n == 1:
                    pe.wait_ge(u_ready, 1)
                tile = 1 - n
                for h in range(H):
                    s = (h % 2) * 4 + h // 2
                    rows = slice((h % 2) * HD, (h % 2 + 1) * HD)
                    per = 512 // keys
                    ins = mm(ps[:, bank + s // per, (s % per) * keys:(s % per + 1) * keys],
                             qT[rows, h // 2, tile * P:(tile + 1) * P], kT[rows, h // 2, 0:keys])
                ins.then_inc(scores, 1)
            pe.wait_ge(pooled_ready, 1)
            pe.wait_ge(wpool_loaded, 16)
            pe.wait_ge(v_ready, 1)
            for g in range(4):
                ins = mm(ps[:, 6 + g // 2, (g % 2) * T:(g % 2 + 1) * T], wpool[:, g, :], mixT[:, 4 + g, :])
            ins.then_inc(ypool_done, 1)
            def project(t, n, chunks):
                for c in chunks:
                    ins = mm(ps[:, 2 * t + n, :], mixT[:, c, t * P:(t + 1) * P],
                             wout[:, c, n * 512:(n + 1) * 512], start=c == 0, stop=c == DC - 1)
                return ins

            pe.wait_ge(ypool_ready, 1)
            pe.wait_ge(wout_loaded, 16)
            pe.wait_ge(masked, 1)
            project(0, 0, range(4))
            project(0, 1, range(4))
            pe.wait_ge(probs, 1)
            pe.wait_ge(masked, 2)
            for n in range(6):
                if n == 4:
                    project(1, 0, range(2))
                    pe.wait_ge(probs, 2)
                    pe.wait_ge(prT_act, 1)
                if n == 5:
                    pe.wait_ge(prT_dve, 1)
                for j in range(4):
                    src = pr0[:, 4 * (n - 4) + j, :] if n >= 4 else pr1[:, 2 * n + j // 2, (j % 2) * P:(j % 2 + 1) * P]
                    ins = pe.transpose(ps[:, 4 + n % 4, j * P:(j + 1) * P], src, c_("ident"))
                ins.then_inc(probs_turned, 1)

            def attend(tile, bank):
                for h in range(H):
                    s = (h % 2) * 4 + h // 2
                    out_ = ps[:, bank + h // 4, (h % 4) * (HD + 1):(h % 4 + 1) * (HD + 1)]
                    for kb in range(tile + 1):
                        src = 2 * s + kb if tile else 2 * H + s
                        ins = mm(out_, prT[:, src, :], vau[:, kb, h, :], start=kb == 0, stop=kb == tile)
                ins.then_inc(attended, 1)

            project(1, 0, range(2, 4))
            pe.wait_ge(prT_act, 2)
            pe.wait_ge(prT_dve, 2)
            pe.wait_ge(pads_ready, 2)
            attend(1, 6)
            pe.wait_ge(prT_act, 3)
            pe.wait_ge(prT_dve, 3)
            attend(0, 4)
            project(1, 1, range(2))
            pe.wait_ge(yat_ready, 2)
            for j in range(4):
                for t in range(TT):
                    ins = pe.transpose(ps[:, 6 + j // 2, (j % 2) * T + t * P:(j % 2) * T + (t + 1) * P],
                                       yat[:, t, j * P:(j + 1) * P], c_("ident"))
            ins.then_inc(yat_turned, 1)
            project(1, 1, range(2, 4))
            pe.wait_ge(ymix_ready, 1)
            pe.wait_ge(ymix_dve, 1)
            project(0, 0, range(4, DC))
            project(0, 1, range(4, DC)).then_inc(projected, 1)
            project(1, 0, range(4, DC)).then_inc(projected, 1)
            def turn_tile(t, half):
                for c in range(4 * half, 4 * half + 4):
                    ins = pe.transpose(ps[:, 4 + 2 * t + half, (c % 4) * P:(c % 4 + 1) * P],
                                       acc[:, t, c * P:(c + 1) * P], c_("ident"))
                ins.then_inc(h2_turned, 1)

            def route(t):
                pe.wait_ge(h2T_act, t + 1)
                pe.wait_ge(h2T_dve, t + 1)
                for c in range(DC):
                    ins = mm(ps[:, t, 0:E], h2T[:, c, t * P:(t + 1) * P], wrt[:, c, :], start=c == 0, stop=c == DC - 1)
                ins.then_inc(logits, 1)

            pe.wait_ge(added, 1)
            turn_tile(0, 0)
            turn_tile(0, 1)
            project(1, 1, range(4, DC)).then_inc(projected, 1)
            pe.wait_ge(half_added, 1)
            turn_tile(1, 0)
            pe.wait_ge(router_loaded, 32)
            route(0)
            pe.wait_ge(added, 2)
            turn_tile(1, 1)
            stay_awake(1)
            route(1)
            stay_awake(3)
            pe.wait_ge(mask_ready, 1)
            both = mask[:].rearrange("p t e -> p (t e)")
            mm(ps[:, 5, 0:2 * E], c_("earlier"), both, stop=False, shared=True)
            mm(ps[:, 5, E:3 * E], c_("ones"), both, start=False, stop=False, shared=True)
            mm(ps[:, 5, 2 * E:3 * E], c_("ones"), mask[:, 0, :], start=False, shared=True).then_inc(ranked, 1)
            pe.wait_ge(comb_ready, 1)
            for t in range(TT):
                ins = pe.transpose(ps[0:E, 4, t * P:(t + 1) * P], comb[:, t, :], c_("ident"))
            ins.then_inc(comb_turned, 1)

            def gather(job):
                bank = ps[:, M[job % 2], :].rearrange("p (e c n) -> p e c n", e=2, c=2)
                for c in (2 * job, 2 * job + 1):
                    for src, first in ((h2h, 2), (h2l, 0)):
                        for t in range(TT):
                            ins = mm(bank[:, :, c % 2], src[:, t, c * P:(c + 1) * P],
                                     disp[:, t, :, first:first + 2, :].rearrange("p e b s -> p e (b s)"),
                                     start=src is h2h and t == 0, stop=src is h2l and t == TT - 1)
                ins.then_inc(gathered, 1)

            def bias(half):
                for n in range(4):
                    rows = slice(n // 2 * 2 * E, (n // 2 + 1) * 2 * E)
                    ins = mm(ps[:, GU + n, :], sel[rows, half, :, :].rearrange("p a s -> p (a s)"),
                             bgu[rows, (n % 2) * 512:(n % 2 + 1) * 512], stop=False)
                ins.then_inc(bias_added, 1)

            def gu_unit(half, c, n, k):
                pe.wait_ge(low_ready, n + 1)
                for b in range(4):
                    for part in range(2):
                        ins = mm(ps[:, GU + b, :], xT[:, half, c].rearrange("p a s -> p (a s)"), split[:, PLACE[k % SPL], part, b * 512:(b + 1) * 512],
                                 start=False, stop=c == GU_U - 1 and part == 1)
                ins.then_inc(unit_used, 1)

            def down_unit(u, n, k):
                pe.wait_ge(low_ready, n + 1)
                for r in range(2):
                    m = 2 * u + r
                    for b in range(2):
                        for part in range(2):
                            col = r * D + b * 512
                            ins = mm(ps[:, Y + b, :], actT[:, m, :, :].rearrange("p a s -> p (a s)"),
                                     split[:, PLACE[k % SPL], part, col:col + 512],
                                     start=m == 0 and part == 0, stop=m == DC - 1 and part == 1)
                ins.then_inc(unit_used, 1)

            def turn_gu(e):
                pe.wait_ge(gu_copied, e + 1)
                for b, done in enumerate((gate_turned, up_turned)):
                    for m in range(DC):
                        ins = mm(ps[:, M[b], m * SLOTS:(m + 1) * SLOTS],
                                 gu[:, b * FE + m * P:b * FE + (m + 1) * P], c_("stack"))
                    ins.then_inc(done, 1)

            def scatter(job):
                t, n = job // 2, job % 2
                for a in range(2):
                    ins = mm(ps[:, M[job % 2], :], dispT[:, a, t, :], ysc[:, a, n * 512:(n + 1) * 512],
                             start=a == 0, stop=a == 1)
                ins.then_inc(scattered, 1)

            pe.wait_ge(sel_ready, 1)
            pe.wait_ge(bgu_ready, 1)
            bias(0)
            pe.wait_ge(disp_ready, 1)
            pe.wait_ge(h2h_ready, 2)
            pe.wait_ge(h2l_ready, 2)
            gather(0)
            gather(1)
            for c in range(GU_U):
                pe.wait_ge(xT_ready, c // 2 + 1)
                gu_unit(0, c, c, c)
                if c in (1, 3):
                    pe.wait_ge(xT_ready, c // 2 + 1)
                    gather(c // 2 + 2)
            pe.wait_ge(bdown_loaded, 16)
            pe.wait_ge(ysc_zeroed, 2)
            pe.wait_ge(identr_ready, 1)
            stay_awake(2, Y)
            turn_gu(0)
            pe.wait_ge(rounds_ready, 1)
            last_pair = pe.snap(pe.value_load(further[0:1, 0:1], min_val=0, max_val=T // SLOTS - 1) * PAIRS + (PAIRS - 1))

            def iteration(i, last):
                def n_(k):
                    return i * ITER_U + PRE_U + k

                pe.wait_ge(gu_copied, i * 2 + 1)
                pe.wait_ge(sel_ready, i * 2 + 2)
                bias(1)
                for k in range(GU_U):
                    gu_unit(1, k, n_(k), PRE_U + k)
                    if k == 1:
                        pe.wait_ge(outputs_ready, i * 2 + 1)
                        pe.wait_ge(gate_clipped, i * 2 + 1)
                        scatter(0)
                        pe.wait_ge(up_clipped, i * 2 + 1)
                        scatter(1)
                    if k == 2:
                        pe.wait_ge(added, i * 4 + TT + 1)
                        scatter(2)
                        pe.wait_ge(added, i * 4 + TT + 2)
                        scatter(3)
                    if k == 3:
                        pe.wait_ge(added, i * 4 + TT + 3)
                        for a in range(2):
                            for t in range(TT):
                                ins = mm(ps[:, M[0], (2 * a + t) * P:(2 * a + t + 1) * P],
                                         disp[:, t, a, 1:3, :].rearrange("p c s -> p (c s)"), identr[:])
                        ins.then_inc(disp_turned, 1)
                    if k == 4:
                        pe.wait_ge(added, i * 4 + TT + 4)
                        pe.wait_ge(pair_taken, i + 1)
                        for a in range(2):
                            for t in range(TT):
                                ins = mm(ps[:, M[1], a:a + 1],
                                         disp[:, t, a, 1:3, :].rearrange("p c s -> p (c s)").bitcast(F32),
                                         cpair[:, t, a:a + 1], start=t == 0, stop=t == TT - 1)
                        ins.then_inc(slots_gated, 1)
                pe.wait_ge(act_ready, i * 2 + 1)
                pe.wait_ge(outputs_ready, i * 2 + 1)
                down_unit(0, n_(8), PRE_U + 8)
                if not last:
                    pe.wait_ge(disp_ready, i + 2)
                    pe.wait_ge(dispT_ready, i + 1)
                    gather(0)
                    pe.wait_ge(gslot_ready, i + 1)
                    gather(1)
                down_unit(1, n_(9), PRE_U + 9)
                if not last:
                    pe.wait_ge(xT_ready, i * 4 + 6)
                turn_gu(i * 2 + 1)
                down_unit(2, n_(10), PRE_U + 10)
                down_unit(3, n_(11), PRE_U + 11)
                if not last:
                    pe.wait_ge(gate_clipped, i * 2 + 2)
                    gather(2)
                    pe.wait_ge(up_clipped, i * 2 + 2)
                    gather(3)
                gap = GU_U if last else 0
                if not last:
                    pe.wait_ge(gu_copied, i * 2 + 2)
                    pe.wait_ge(sel_ready, i * 2 + 3)
                    bias(0)
                    pe.wait_ge(xT_ready, i * 4 + 8)
                    for k in range(GU_U):
                        gu_unit(0, k, n_(12 + k), PRE_U + 12 + k)
                if last:
                    pe.wait_ge(outputs_ready, i * 2 + 2)
                    pe.wait_ge(gu_copied, i * 2 + 2)
                    last_scatter(0)
                pe.wait_ge(act_ready, i * 2 + 2)
                pe.wait_ge(outputs_ready, i * 2 + 2)
                for u in range(DN_U):
                    down_unit(u, n_(20 + u - gap), PRE_U + 20 + u - gap)
                    if u == 1 and not last:
                        turn_gu(i * 2 + 2)

            def last_scatter(a):
                for job in range(4):
                    ins = mm(ps[:, job, :], dispT[:, a, job // 2, :], ysc[:, a, (job % 2) * 512:(job % 2 + 1) * 512],
                             start=a == 0, stop=a == 1)
                    if a == 1:
                        ins.then_inc(scattered, 1)

            with pe.Fori(0, last_pair) as i:
                iteration(i, False)
            iteration(last_pair, True)
            pe.wait_ge(outputs_ready, last_pair * 2 + 4)
            last_scatter(1)


_INS = ["x", "g_mix", "w_in", "w_pool", "pool_scale", "w_out", "g_ffn", "w_router", "b_router",
        "w_gu", "b_gu", "w_down", "b_down", "g_final"]


def kernel(**inputs):
    import concourse.bacc as bacc
    from concourse.bass_utils import run_bass_kernel_spmd

    nc = bacc.Bacc("TRN2", target_bir_lowering=False, num_devices=1)
    arrays, args = {}, []
    for name in _INS + ["consts"]:
        a = np.ascontiguousarray(constants() if name == "consts" else inputs[name])
        arrays[f"in_{name}"] = a
        args.append(nc.dram_tensor(f"in_{name}", a.shape, mybir.dt.from_np(a.dtype), kind="ExternalInput").ap())
    args.append(nc.dram_tensor("out", (1, T, D), F32, kind="ExternalOutput").ap())
    hybrid_layer(nc, *args)
    r = run_bass_kernel_spmd(nc, [arrays], core_ids=[0])
    return r.results[0]["out"]
```
